# Optimizing a Trainium2 kernel written in Bass

```python
import math
import jax, jax.numpy as jnp
from jax import lax
import numpy as np

D_MODEL = 1024
BATCH = 1
SEQ = 512
DEPTH = 2

CTX_LEN = 256
GRID_W = 64
N_EVEN = (DEPTH + 1) // 2
N_ODD = DEPTH // 2
N_MOD = 9
D_FF = 2816
NORM_EPS = 1e-6
NEG_INF = -1e30
ROPE_BASE = 10000.0
NA_HEADS = 8
NA_HD = 64
NA_WIN_H = 8
NA_WIN_W = 16
NA_QB_W = 16
NA_KB_W = NA_QB_W + NA_WIN_W
NA_PROJ = 3 * NA_HEADS * NA_HD
DN_HEADS = 4
DN_DK = 128
DN_DV = 128
DN_CONV = 5
DN_CHUNK = 64
DN_QKV = DN_HEADS * (2 * DN_DK + DN_DV)
DN_PROJ = DN_QKV + DN_HEADS * DN_DV + 4 * DN_HEADS
EVEN_PROJ = NA_PROJ + DN_PROJ
EVEN_MIX_W = NA_HEADS * NA_HD + DN_HEADS * DN_DV
SWA_HEADS = 16
SWA_KV_HEADS = 4
SWA_HD = 64
SWA_WINDOW = 128
SWA_BLOCK = 128
ODD_PROJ = (SWA_HEADS + 2 * SWA_KV_HEADS) * SWA_HD
ODD_MIX_W = SWA_HEADS * SWA_HD

kernel_name = "hybrid_na_deltanet_swa_prefix_dit"

def rmsnorm(x, g):
    xf = x.astype(jnp.float32)
    y = xf * lax.rsqrt(jnp.mean(xf * xf, -1, keepdims=True) + NORM_EPS)
    return (y * g.astype(jnp.float32)).astype(x.dtype)

def l2norm(x):
    xf = x.astype(jnp.float32)
    return (xf * lax.rsqrt(jnp.sum(xf * xf, -1, keepdims=True) + NORM_EPS)).astype(x.dtype)

def modulate(h, g, shift, scale):
    return rmsnorm(h, g) * (1 + scale) + shift

def adaln_terms(s, w, b):
    return jnp.split(jax.nn.silu(s) @ w + b, N_MOD, -1)

def swiglu(x, w_up, w_down):
    gate, up = jnp.split(x @ w_up, 2, -1)
    return (jax.nn.silu(gate) * up) @ w_down

def axial_rope_tables(T):
    t = jnp.arange(T)
    half = SWA_HD // 2
    inv = jnp.power(ROPE_BASE, -jnp.arange(0, half, 2, dtype=jnp.float32) / half)
    ang_r = (t // GRID_W).astype(jnp.float32)[:, None] * inv
    ang_c = (t % GRID_W).astype(jnp.float32)[:, None] * inv
    return (jnp.cos(ang_r)[:, None, :], jnp.sin(ang_r)[:, None, :],
            jnp.cos(ang_c)[:, None, :], jnp.sin(ang_c)[:, None, :])

def rope_half(x, cos, sin):
    x1, x2 = jnp.split(x.astype(jnp.float32), 2, -1)
    return jnp.concatenate([x1 * cos - x2 * sin, x2 * cos + x1 * sin], -1)

def axial_rope(x, tabs):
    cr, sr, cc, sc = tabs
    xr, xc = jnp.split(x, 2, -1)
    return jnp.concatenate([rope_half(xr, cr, sr), rope_half(xc, cc, sc)], -1).astype(x.dtype)

def context_attention(qc, kc, vc, sink=None):
    B, Tc = qc.shape[:2]
    s = jnp.einsum('bqgrd,bkgd->bgrqk', qc, kc).astype(jnp.float32) * qc.shape[-1] ** -0.5
    if sink is not None:
        s = jnp.concatenate([s, jnp.broadcast_to(sink.astype(jnp.float32)[None, :, :, None, None], s.shape[:-1] + (1,))], -1)
    p = jax.nn.softmax(s, -1)[..., :kc.shape[1]].astype(vc.dtype)
    return jnp.einsum('bgrqk,bkgd->bqgrd', p, vc).reshape(B, Tc, -1)

def neighbourhood_attention(q, k, v, kc, vc, rpb):
    B, T, H, d = q.shape
    rows = T // GRID_W
    kh = min(NA_WIN_H, rows)
    ncb = GRID_W // NA_QB_W
    nwin = kh * NA_KB_W
    jb = jnp.arange(ncb)
    cidx = jnp.clip(jb * NA_QB_W - NA_WIN_W // 2, 0, GRID_W - NA_KB_W)[:, None] + jnp.arange(NA_KB_W)[None, :]
    qcol = jb[:, None] * NA_QB_W + jnp.arange(NA_QB_W)[None, :]
    cstart = jnp.clip(qcol - NA_WIN_W // 2, 0, GRID_W - NA_WIN_W)
    col_ok = (cidx[:, None, :] >= cstart[:, :, None]) & (cidx[:, None, :] < cstart[:, :, None] + NA_WIN_W)
    dc = jnp.clip(cidx[:, None, :] - qcol[:, :, None] + NA_WIN_W - 1, 0, 2 * NA_WIN_W - 2)
    kgrid = k.reshape(B, rows, GRID_W, H, d)
    vgrid = v.reshape(B, rows, GRID_W, H, d)
    q_rows = jnp.moveaxis(q.reshape(B, rows, ncb, NA_QB_W, H, d), 1, 0)
    rpb_f = rpb.astype(jnp.float32)
    scale = d ** -0.5

    def row_block(args):
        r, q_r = args
        r0 = jnp.clip(r - kh // 2, 0, rows - kh)
        k_r = lax.dynamic_slice_in_dim(kgrid, r0, kh, axis=1)[:, :, cidx]
        v_r = lax.dynamic_slice_in_dim(vgrid, r0, kh, axis=1)[:, :, cidx]
        dr = r0 + jnp.arange(kh) - r + NA_WIN_H - 1
        bias = rpb_f[:, dr[None, None, :, None], dc[:, :, None, :]]
        s_win = jnp.einsum('bjqhd,bajkhd->bhjqak', q_r, k_r).astype(jnp.float32) * scale + bias
        s_win = jnp.where(col_ok[:, :, None, :], s_win, NEG_INF).reshape(B, H, ncb, NA_QB_W, nwin)
        s_ctx = jnp.einsum('bjqhd,bchd->bhjqc', q_r, kc).astype(jnp.float32) * scale
        p = jax.nn.softmax(jnp.concatenate([s_win, s_ctx], -1), -1).astype(v.dtype)
        p_win = p[..., :nwin].reshape(B, H, ncb, NA_QB_W, kh, NA_KB_W)
        o = jnp.einsum('bhjqak,bajkhd->bjqhd', p_win, v_r) + jnp.einsum('bhjqc,bchd->bjqhd', p[..., nwin:], vc)
        return o.reshape(B, GRID_W, H * d)

    o = lax.map(row_block, (jnp.arange(rows), q_rows))
    return jnp.moveaxis(o, 0, 1).reshape(B, T, H * d)

def centred_short_conv(x, w):
    K = w.shape[0]
    T = x.shape[1]
    xp = jnp.pad(x, ((0, 0), (K // 2, K // 2), (0, 0)))
    return jax.nn.silu(sum(xp[:, j:j + T] * w[j] for j in range(K)))

def chunk_gated_delta_rule(q, k, v, g, beta, S0):
    B, T, H, dk = k.shape
    dv = v.shape[-1]
    C = DN_CHUNK
    N = T // C

    def chunks(t):
        return jnp.moveaxis(t.astype(jnp.float32).reshape((B, N, C) + t.shape[2:]), 3, 2)

    q = chunks(q) * dk ** -0.5
    k = chunks(k)
    v = chunks(v)
    beta = chunks(beta)
    g = jnp.cumsum(chunks(g), -1)
    idx = jnp.arange(C)
    incl = idx[:, None] >= idx[None, :]
    strict = idx[:, None] > idx[None, :]
    diff = g[..., :, None] - g[..., None, :]
    decay = jnp.where(incl, jnp.exp(jnp.where(incl, diff, 0.0)), 0.0)
    kb = k * beta[..., None]
    L = jnp.where(strict, jnp.einsum('bnhcd,bnhsd->bnhcs', kb, k) * decay, 0.0)
    A = L + jnp.eye(C, dtype=jnp.float32)
    rhs = jnp.concatenate([v * beta[..., None], kb * jnp.exp(g)[..., None]], -1)
    sol = lax.linalg.triangular_solve(A, rhs, left_side=True, lower=True, unit_diagonal=True)
    u, w = sol[..., :dv], sol[..., dv:]
    qk = jnp.einsum('bnhcd,bnhsd->bnhcs', q, k) * decay
    q_dec = q * jnp.exp(g)[..., None]
    k_dec = k * jnp.exp(g[..., -1:] - g)[..., None]
    g_last = jnp.exp(g[..., -1])

    def step(S, xs):
        q_i, k_i, u_i, w_i, qk_i, gl = xs
        v_new = u_i - jnp.einsum('bhcd,bhde->bhce', w_i, S)
        o = jnp.einsum('bhcd,bhde->bhce', q_i, S) + jnp.einsum('bhcs,bhse->bhce', qk_i, v_new)
        S = S * gl[..., None, None] + jnp.einsum('bhcd,bhce->bhde', k_i, v_new)
        return S, o

    xs = tuple(jnp.moveaxis(t, 1, 0) for t in (q_dec, k_dec, u, w, qk, g_last))
    S, o = lax.scan(step, S0.astype(jnp.float32), xs)
    o = jnp.moveaxis(jnp.moveaxis(o, 0, 1), 2, 3).reshape(B, T, H, dv)
    return o, S

def gated_rmsnorm(o, z, w):
    of = o.astype(jnp.float32)
    y = of * lax.rsqrt(jnp.mean(of * of, -1, keepdims=True) + NORM_EPS) * w.astype(jnp.float32) * jax.nn.silu(z.astype(jnp.float32))
    return y.astype(z.dtype).reshape(z.shape[0], z.shape[1], -1)

def maybe_flip(t, d):
    return jnp.flip(t, 1) if d else t

def gated_deltanet(p, pc, conv_w, a_log, dt_bias, norm_w, need_ctx):
    def prep(t):
        B, T, _ = t.shape
        qkv = centred_short_conv(t[..., :DN_QKV], conv_w)
        q, k, v = jnp.split(qkv, [DN_HEADS * DN_DK, 2 * DN_HEADS * DN_DK], -1)
        q = l2norm(q.reshape(B, T, DN_HEADS, DN_DK))
        k = l2norm(k.reshape(B, T, DN_HEADS, DN_DK))
        v = v.reshape(B, T, DN_HEADS, DN_DV)
        z = t[..., DN_QKV:DN_QKV + DN_HEADS * DN_DV].reshape(B, T, DN_HEADS, DN_DV)
        ab = t[..., DN_QKV + DN_HEADS * DN_DV:].astype(jnp.float32).reshape(B, T, 2, 2, DN_HEADS)
        g = -jnp.exp(a_log.astype(jnp.float32)) * jax.nn.softplus(ab[:, :, 0] + dt_bias.astype(jnp.float32))
        beta = jax.nn.sigmoid(ab[:, :, 1])
        return q, k, v, z, g, beta

    q, k, v, z, g, beta = prep(p)
    qc, kc, vc, zc, gc, betac = prep(pc)
    B = p.shape[0]
    S0 = jnp.zeros((B, DN_HEADS, DN_DK, DN_DV), jnp.float32)
    o = 0.0
    o_c = 0.0
    for d in range(2):
        oc_d, S_ctx = chunk_gated_delta_rule(maybe_flip(qc, d), maybe_flip(kc, d), maybe_flip(vc, d),
                                             maybe_flip(gc[:, :, d], d), maybe_flip(betac[:, :, d], d), S0)
        o_d, _ = chunk_gated_delta_rule(maybe_flip(q, d), maybe_flip(k, d), maybe_flip(v, d),
                                        maybe_flip(g[:, :, d], d), maybe_flip(beta[:, :, d], d), S_ctx)
        o = o + maybe_flip(o_d, d)
        if need_ctx:
            o_c = o_c + maybe_flip(oc_d, d)
    out = gated_rmsnorm(o, z, norm_w)
    out_c = gated_rmsnorm(o_c, zc, norm_w) if need_ctx else None
    return out, out_c

def even_mixer(u, uc, w_in, w_out, rpb, conv_w, a_log, dt_bias, dn_norm_w, need_ctx):
    B, T, _ = u.shape
    Tc = uc.shape[1]
    p = u @ w_in
    pc = uc @ w_in
    q, k, v = [t.reshape(B, T, NA_HEADS, NA_HD) for t in jnp.split(p[..., :NA_PROJ], 3, -1)]
    qc, kc, vc = [t.reshape(B, Tc, NA_HEADS, NA_HD) for t in jnp.split(pc[..., :NA_PROJ], 3, -1)]
    y_na = neighbourhood_attention(q, k, v, kc, vc, rpb)
    y_dn, y_dn_c = gated_deltanet(p[..., NA_PROJ:], pc[..., NA_PROJ:], conv_w, a_log, dt_bias, dn_norm_w, need_ctx)
    y = jnp.concatenate([y_na, y_dn], -1) @ w_out
    if not need_ctx:
        return y, None
    y_na_c = context_attention(qc[:, :, :, None, :], kc, vc)
    yc = jnp.concatenate([y_na_c, y_dn_c], -1) @ w_out
    return y, yc

def windowed_gqa_sink(q, k, v, kc, vc, sink):
    B, T, Hq, d = q.shape
    G = k.shape[2]
    R = Hq // G
    nb = T // SWA_BLOCK
    pad = ((0, 0), (SWA_BLOCK, SWA_BLOCK), (0, 0), (0, 0))
    kp = jnp.pad(k, pad)
    vp = jnp.pad(v, pad)
    qb = jnp.moveaxis(q.reshape(B, nb, SWA_BLOCK, G, R, d), 1, 0)
    qi = jnp.arange(SWA_BLOCK)
    ki = jnp.arange(3 * SWA_BLOCK) - SWA_BLOCK
    rel = ki[None, :] - qi[:, None]
    sink_f = sink.astype(jnp.float32).reshape(G, R)
    scale = d ** -0.5
    nwin = 3 * SWA_BLOCK
    Tc = kc.shape[1]

    def block(args):
        n, q_n = args
        k_n = lax.dynamic_slice_in_dim(kp, n * SWA_BLOCK, nwin, axis=1)
        v_n = lax.dynamic_slice_in_dim(vp, n * SWA_BLOCK, nwin, axis=1)
        kpos = n * SWA_BLOCK + ki
        ok = (jnp.abs(rel) <= SWA_WINDOW) & ((kpos >= 0) & (kpos < T))[None, :]
        s_win = jnp.where(ok, jnp.einsum('bqgrd,bkgd->bgrqk', q_n, k_n).astype(jnp.float32) * scale, NEG_INF)
        s_ctx = jnp.einsum('bqgrd,bcgd->bgrqc', q_n, kc).astype(jnp.float32) * scale
        s_sink = jnp.broadcast_to(sink_f[None, :, :, None, None], s_ctx.shape[:-1] + (1,))
        p = jax.nn.softmax(jnp.concatenate([s_win, s_ctx, s_sink], -1), -1).astype(v.dtype)
        o = (jnp.einsum('bgrqk,bkgd->bqgrd', p[..., :nwin], v_n)
             + jnp.einsum('bgrqc,bcgd->bqgrd', p[..., nwin:nwin + Tc], vc))
        return o.reshape(B, SWA_BLOCK, Hq * d)

    o = lax.map(block, (jnp.arange(nb), qb))
    return jnp.moveaxis(o, 0, 1).reshape(B, T, Hq * d)

def odd_mixer(u, uc, w_in, w_out, sink, rope, need_ctx):
    B, T, _ = u.shape
    Tc = uc.shape[1]
    QW = SWA_HEADS * SWA_HD
    KW = SWA_KV_HEADS * SWA_HD
    R = SWA_HEADS // SWA_KV_HEADS
    p = u @ w_in
    q = axial_rope(p[..., :QW].reshape(B, T, SWA_HEADS, SWA_HD), rope)
    k = axial_rope(p[..., QW:QW + KW].reshape(B, T, SWA_KV_HEADS, SWA_HD), rope)
    v = p[..., QW + KW:].reshape(B, T, SWA_KV_HEADS, SWA_HD)
    kvc = uc @ w_in[:, QW:]
    kc = kvc[..., :KW].reshape(B, Tc, SWA_KV_HEADS, SWA_HD)
    vc = kvc[..., KW:].reshape(B, Tc, SWA_KV_HEADS, SWA_HD)
    y = windowed_gqa_sink(q, k, v, kc, vc, sink) @ w_out
    if not need_ctx:
        return y, None
    qc = (uc @ w_in[:, :QW]).reshape(B, Tc, SWA_KV_HEADS, R, SWA_HD)
    yc = context_attention(qc, kc, vc, sink.reshape(SWA_KV_HEADS, R)) @ w_out
    return y, yc

def setup_inputs(seed: int = 0) -> dict:
    key = jax.random.key(seed)
    ks = jax.random.split(key, 20)
    f32 = jnp.float32

    def nrm(k, shape, fan_in, gain=1.0):
        return jax.random.normal(k, shape, f32) * (gain * fan_in ** -0.5)

    dt = jnp.exp(jax.random.uniform(ks[14], (N_EVEN, 2, DN_HEADS), f32, math.log(1e-3), math.log(1e-1)))
    return {
        "x": jax.random.normal(ks[0], (BATCH, SEQ, D_MODEL), f32),
        "c": jax.random.normal(ks[1], (BATCH, D_MODEL), f32),
        "ctx": jax.random.normal(ks[2], (BATCH, CTX_LEN, D_MODEL), f32),
        "c_ctx": jax.random.normal(ks[3], (D_MODEL,), f32),
        "ada_w": nrm(ks[4], (DEPTH, D_MODEL, N_MOD * D_MODEL), D_MODEL, 0.5),
        "ada_b": 0.02 * jax.random.normal(ks[5], (DEPTH, N_MOD * D_MODEL), f32),
        "norm_g": 1.0 + 0.02 * jax.random.normal(ks[6], (DEPTH, 3, D_MODEL), f32),
        "ffn_w_up": nrm(ks[7], (DEPTH, 2, D_MODEL, 2 * D_FF), D_MODEL),
        "ffn_w_down": nrm(ks[8], (DEPTH, 2, D_FF, D_MODEL), D_FF),
        "even_w_in": nrm(ks[9], (N_EVEN, D_MODEL, EVEN_PROJ), D_MODEL),
        "even_w_out": nrm(ks[10], (N_EVEN, EVEN_MIX_W, D_MODEL), EVEN_MIX_W),
        "na_rpb": 0.1 * jax.random.normal(ks[11], (N_EVEN, NA_HEADS, 2 * NA_WIN_H - 1, 2 * NA_WIN_W - 1), f32),
        "dn_conv_w": nrm(ks[12], (N_EVEN, DN_CONV, DN_QKV), DN_CONV),
        "dn_a_log": jnp.log(jax.random.uniform(ks[13], (N_EVEN, 2, DN_HEADS), f32, 1.0, 16.0)),
        "dn_dt_bias": dt + jnp.log(-jnp.expm1(-dt)),
        "dn_norm_w": 1.0 + 0.02 * jax.random.normal(ks[15], (N_EVEN, DN_DV), f32),
        "odd_w_in": nrm(ks[16], (N_ODD, D_MODEL, ODD_PROJ), D_MODEL),
        "odd_w_out": nrm(ks[17], (N_ODD, ODD_MIX_W, D_MODEL), ODD_MIX_W),
        "swa_sink": jax.random.normal(ks[18], (N_ODD, SWA_HEADS), f32),
        "final_norm_g": 1.0 + 0.02 * jax.random.normal(ks[19], (D_MODEL,), f32),
    }

def reference(x, c, ctx, c_ctx, ada_w, ada_b, norm_g, ffn_w_up, ffn_w_down, even_w_in, even_w_out, na_rpb,
              dn_conv_w, dn_a_log, dn_dt_bias, dn_norm_w, odd_w_in, odd_w_out, swa_sink, final_norm_g):
    T = x.shape[1]
    rope = axial_rope_tables(T)
    h, hc = x, ctx
    for i in range(DEPTH):
        need_ctx = i < DEPTH - 1
        j = i // 2
        ml = adaln_terms(c[:, None, :], ada_w[i], ada_b[i])
        mc = adaln_terms(c_ctx, ada_w[i], ada_b[i])
        h = h + 0.5 * ml[2] * swiglu(modulate(h, norm_g[i, 0], ml[0], ml[1]), ffn_w_up[i, 0], ffn_w_down[i, 0])
        hc = hc + 0.5 * mc[2] * swiglu(modulate(hc, norm_g[i, 0], mc[0], mc[1]), ffn_w_up[i, 0], ffn_w_down[i, 0])
        u = modulate(h, norm_g[i, 1], ml[3], ml[4])
        uc = modulate(hc, norm_g[i, 1], mc[3], mc[4])
        if i % 2 == 0:
            y, yc = even_mixer(u, uc, even_w_in[j], even_w_out[j], na_rpb[j], dn_conv_w[j], dn_a_log[j],
                               dn_dt_bias[j], dn_norm_w[j], need_ctx)
        else:
            y, yc = odd_mixer(u, uc, odd_w_in[j], odd_w_out[j], swa_sink[j], rope, need_ctx)
        h = h + ml[5] * y
        h = h + 0.5 * ml[8] * swiglu(modulate(h, norm_g[i, 2], ml[6], ml[7]), ffn_w_up[i, 1], ffn_w_down[i, 1])
        if need_ctx:
            hc = hc + mc[5] * yc
            hc = hc + 0.5 * mc[8] * swiglu(modulate(hc, norm_g[i, 2], mc[6], mc[7]), ffn_w_up[i, 1], ffn_w_down[i, 1])
    return rmsnorm(h, final_norm_g)


_drawn_inputs = setup_inputs


def setup_inputs(seed=0):
    import zlib

    import numpy as np

    out = dict(_drawn_inputs(seed))
    spreads = {}
    factors = {'norm_g': 7.243,
     'na_rpb': 23.609,
     'dn_norm_w': 8.0,
     'swa_sink': 8.0,
     'final_norm_g': 8.127}
    for name, (base, spread) in spreads.items():
        noise = np.random.default_rng([zlib.crc32(name.encode()), seed]).standard_normal(out[name].shape)
        drawn = base * np.exp(spread * noise) if base else spread * noise
        out[name] = __import__('jax').numpy.asarray(drawn.astype(out[name].dtype))
    for name, factor in factors.items():
        out[name] = (out[name] * factor).astype(out[name].dtype)
    return out
```

```python
import numpy as np
import concourse.bass as bass
from concourse import mybir
from contextlib import ExitStack

D = 1024
T_LAT, T_CTX = 512, 256
T = T_LAT + T_CTX
P = 128
KD = D // P
DEPTH = 2
N_MOD = 9
D_FF = 2816
FFC = D_FF // P
PARTS = [8, 7, 7]
EPS = 1e-6
LAT, CTX = (0, T_LAT), (T_LAT, T)
NA_HEADS, DN_HEADS, SWA_HEADS, SWA_KV = 8, 4, 16, 4
HD = 64
GRID_W, ROWS = 64, T_LAT // 64
NA_PROJ = 3 * NA_HEADS * HD
DN_QKV = DN_HEADS * 3 * P
CONV = 5

RAW_SLOTS, SPLIT_SLOTS, ADA_SLOTS = 4, 3, 2
NEG = -1e30
PAIRS = 4


def segments(layer, f):
    return [LAT] if (layer, f) == (DEPTH - 1, 1) else [LAT, CTX]


def ffn_products(layer, f):
    items = []
    j = 0
    for part, n in enumerate(PARTS):
        for c in range(n):
            items += [("gate", layer, f, part, c, j), ("up", layer, f, part, c, j)]
            j += 1
        items += [("down", layer, f, part, i) for i in range(KD)]
    return items


def insert_before(items, match, extra):
    at = next(i for i, x in enumerate(items) if x[:len(match)] == match)
    return items[:at] + extra + items[at:]


def schedule(mixers=True):
    s = [("ada", 0, 0), ("ada", 0, 1), ("norm", 0)]
    f = ffn_products(0, 0)
    f = insert_before(f, ("down", 0, 0, 0), [("ada", 0, 2)])
    f = insert_before(f, ("gate", 0, 0, 1), [("ada", 0, 3), ("ada", 0, 4)])
    f = insert_before(f, ("gate", 0, 0, 2), [("ada", 0, 5), ("ada", 0, 6)])
    f = f + [("ada", 0, 7), ("ada", 0, 8)]
    s += f
    if mixers:
        s += even_products()
    s += [("ada", 1, t) for t in range(9)] if not mixers else []
    s += [("norm", 2)] + ffn_products(0, 1) + [("norm", 3)] + ffn_products(1, 0)
    if mixers:
        s += odd_products()
    s += [("norm", 5)] + ffn_products(1, 1) + [("norm", 6)]
    return s


SCAN = [[4, 5, 0, 1, 2, 3], [5, 4, 3, 2, 1, 0]]
STEPS = T // P
LEVELS = 7


def attention_products(layer, units, values_before):
    items = []
    for u in units + [None]:
        if u is not None:
            items += [("S", u, 0), ("S", u, 1)]
        if u != units[0]:
            p = units[-1] if u is None else u - 1
            items += values_before.get(p, []) + [("PT", p, 0), ("PT", p, 1), ("O", p)]
            if last_of_block(p):
                items.append(("Y", block_of(p)))
    return items


def block_of(u):
    return u // 4 if u < 24 else 6 + (u - 24) // 8


def last_of_block(u):
    return u % 4 == 3 if u < 24 else (u - 24) % 8 == 7


def even_products():
    s = [("norm", 1)]
    s += [("proj", 0, w, i) for w in ("dq", "dk", "dv") for i in range(4)] + [("proj", 0, "ab", 0)]
    s += [("proj", 0, "z", i) for i in range(4)]
    norms = [("l2", w, i) for w in ("dq", "dk") for i in range(4)]
    for i, x in enumerate([("proj", 0, w, i) for w in ("nq", "nk", "nv") for i in range(4)]):
        s += [x] + norms[i:i + 1]
    s += [("cum",)]
    ada = [("ada", 1, t) for t in range(9)]
    for st in range(STEPS):
        both = lambda kind, *r: [(kind, st, d, *r) for d in range(2)]
        s += both("dnA") + both("dnT")
        for k in range(1, LEVELS):
            s += both("dnN", k) + both("dnY", k) + (both("dnX", k) if k < LEVELS - 1 else [])
        s += both("dnV") + (both("dnK") if st else []) + ada[:1]
        s += both("dnU") + ada[1:2] + both("dnO")
        ada = ada[2:]
    s += [("dny", t) for t in range(STEPS)]
    before = {4 * jb: [("vt", 0, jb)] for jb in range(4)}
    before[0] = [("vt", 0, 4)] + before[0]
    s += attention_products(0, list(range(24)), before)
    return s + [("out", 0, i) for i in range(KD)]


def odd_products():
    s = [("norm", 4)]
    order = [("proj", 1, w, i) for w, n in (("k", 2), ("q", 8)) for i in range(n)]
    for i, x in enumerate(order):
        s.append(x)
        if i:
            s.append(("rope", i - 1))
        if i == 1:
            s += [("proj", 1, "v", 0), ("proj", 1, "v", 1)]
    s += [("rope", len(order) - 1), ("vt", 1, 0), ("vt", 1, 1)]
    s += attention_products(1, list(range(24, 56)), {})
    return s + [("out", 1, i) for i in range(KD)]


RESIDUAL = ("down", "out")


def weight_slots(items):
    out = []
    for x in items:
        if x[0] in ("gate", "up", "out", "proj"):
            out.append((x, KD, 16 if x[2] == "ab" else P))
        elif x[0] == "down":
            out.append((x, PARTS[x[3]], P))
    return out


def build(nc, a, out, items):
    f32, f32r = mybir.dt.float32, mybir.dt.float32r
    ALU, ACT = mybir.AluOpType, mybir.ActivationFunctionType

    slots = weight_slots(items)
    slot_of = {x: n for n, (x, _, _) in enumerate(slots)}
    slot_at = np.concatenate([[0], np.cumsum([P * k * w for _, k, w in slots])]).tolist()
    number = {x: i for i, x in enumerate(items)}
    ada_order = [x for x in items if x[0] == "ada"]
    ada_no = {x: i for i, x in enumerate(ada_order)}
    norm_no = {x: i for i, x in enumerate([x for x in items if x[0] == "norm"])}
    glu_no = {x[1:]: i for i, x in enumerate([x for x in items if x[0] == "up"])}
    no = {kind: {x: i for i, x in enumerate([x for x in items if x[0] == kind])} for kind in {x[0] for x in items}}
    conv_no = {x: i for i, x in enumerate([x for x in items if x[0] == "proj" and x[2] in ("dq", "dk", "dv")])}
    stage_no = {x: i for i, x in enumerate([x for x in items if x[0] == "proj" and x[2] in ("z", "nq", "nk", "nv")])}
    odd_no = {x: i for i, x in enumerate([x for x in items if x[0] == "proj" and x[1] == 1])}
    res_no = {x: i for i, x in enumerate([x for x in items if x[0] in RESIDUAL])}
    squares = {}
    residuals = []
    for x in items:
        if x[0] in RESIDUAL:
            residuals.append(x)
        elif x[0] == "norm" and residuals:
            for i, y in enumerate(residuals[-KD:]):
                squares[y] = (norm_no[x], i)
    norm_items = [x for x in items if x[0] == "norm"]
    final = norm_items[-1]

    with ExitStack() as ctx:
        def sb(name, shape, dt=f32):
            return ctx.enter_context(nc.sbuf_tensor(name, shape, dt))

        def sem(name):
            return ctx.enter_context(nc.semaphore(name))

        h = sb("h", [P, KD, T])
        raw = [sb(f"raw{i}", [P, KD * P]) for i in range(RAW_SLOTS)]
        wh = [sb(f"wh{i}", [P, KD * P], f32r) for i in range(SPLIT_SLOTS)]
        wl = [sb(f"wl{i}", [P, KD * P], f32r) for i in range(SPLIT_SLOTS)]
        ada_raw = [sb(f"ada_raw{i}", [P, KD * P]) for i in range(ADA_SLOTS)]
        sc = sb("sc", [P, KD, 2])
        ada_b = sb("ada_b", [P, DEPTH, N_MOD, KD])
        norm_g = sb("norm_g", [P, DEPTH * 3 + 1, KD])
        ada_tmp = sb("ada_tmp", [P, KD, 2])
        mod = sb("mod", [P, DEPTH, N_MOD, KD, 2])
        mean_w = sb("mean_w", [P, P])
        ones_w = sb("ones_w", [P, P])
        ident = sb("ident", [P, P])
        eps = sb("eps", [P, 1])
        rows = sb("rows", [P, 40])
        conv_w = sb("conv_w", [P, 12, CONV])
        dn_w = sb("dn_w", [P, 1])
        sq = [sb(f"sq{i}", [P, T]) for i in range(2)]
        sumsq = sb("sumsq", [P, T])
        std = sb("std", [P, T])
        rstd = sb("rstd", [P, T])
        nsink = sb("nsink", [P, 16])
        smx, snb, sden, ses, srec = (sb(n, [P, 56, 2]) for n in ("smx", "snb", "sden", "ses", "srec"))

        def region(name):
            guard = ExitStack()
            return guard, lambda n, shape, dt=f32: guard.enter_context(nc.sbuf_tensor(n, shape, dt))

        guard_u, ub = region("u")
        uh = ub("uh", [P, KD, T], f32r)
        ul = ub("ul", [P, KD, T], f32r)
        guard, fb = region("ffn")
        ah = fb("ah", [P, KD, T], f32r)
        al = fb("al", [P, KD, T], f32r)
        sg = [fb(f"sg{i}", [P, T]) for i in range(2)]
        af = [fb(f"af{i}", [P, T]) for i in range(2)]
        guard.close()
        guard, db = region("deltanet")
        dqkv = db("dqkv", [P, 3, DN_HEADS, T])
        o_acc = db("o_acc", [P, STEPS, 4 * P])
        masks = db("masks", [P, 4 + 2 * LEVELS, P])
        cacc = [db(f"cacc{i}", [P, T]) for i in range(2)]
        n_small = STEPS * 8
        ab, decay, beta, gc, eg, nbe, kdec, egl = (db(n, [P, STEPS, 16 if n == "ab" else 8])
                                               for n in ("ab", "g", "beta", "gc", "eg", "nbe", "kdec", "egl"))
        sp_a, sp_e, ea = db("sp_a", [P, STEPS, 8]), db("sp_e", [P, STEPS, 8]), db("ea", [P, 8])
        oss = db("oss", [P, STEPS, 4])
        guard.close()
        guard, nb = region("neighbourhood")
        nqkv = nb("nqkv", [P, 3, 4, T])
        vblk = nb("vblk", [P, 2, 4 * P])
        vctx = nb("vctx", [P, 2, 4 * P])
        bias = [nb(f"bias{i}", [P, 2, 2 * P]) for i in range(2)]
        prob_e = [nb(f"prob_e{i}", [P, 4 * P]) for i in range(4)]
        probT_e = [nb(f"probT_e{i}", [P, 4 * P]) for i in range(2)]
        otok_e = [nb(f"otok_e{i}", [P, 4 * P]) for i in range(2)]
        guard.close()
        guard, ob = region("windowed")
        sq_q = ob("sq_q", [P, KD, T_LAT])
        sw_k, sw_v = ob("sw_k", [P, 2, T]), ob("sw_v", [P, 2, T])
        sw_vt = ob("sw_vt", [P, STEPS, 2 * P])
        rope_c, rope_s = ob("rope_c", [P, T_LAT]), ob("rope_s", [P, T_LAT])
        rope_x = [ob(f"rope_x{i}", [P, T_LAT]) for i in range(2)]
        rope_p = ob("rope_p", [P, P])
        wmask = ob("wmask", [P, 2, P])
        prob_o = [ob(f"prob_o{i}", [P, 5 * P]) for i in range(4)]
        probT_o = [ob(f"probT_o{i}", [P, 5 * P]) for i in range(2)]
        otok_o = [ob(f"otok_o{i}", [P, KD * P]) for i in range(2)]
        guard.close()
        guard_u.close()
        guard, wb = region("deltanet work")
        dE, dEM, dEQ, dA, dAT, dX, dY, dN, dQK, dVb, dKd, dS = (
            [wb(f"{n}{d}", [P, 4, P]) for d in range(2)]
            for n in ("dE", "dEM", "dEQ", "dA", "dAT", "dX", "dY", "dN", "dQK", "dVb", "dKd", "dS"))
        guard.close()
        dR, dQS, dVn = dE, dEM, dEQ
        zt = [std[:, 0:4 * P], rstd[:, 0:4 * P]]
        m8 = std[:, :].rearrange("p (b k) -> p b k", b=3)
        scratch = nc.dram_tensor("spill", (16, P, T), f32, kind="Internal").ap()
        toeplitz = nc.dram_tensor("toeplitz", (16, NA_HEADS, 15, 48), f32, kind="Internal").ap()
        bias_hbm = nc.dram_tensor("bias_hbm", (3, NA_HEADS, ROWS, 16, ROWS, 32), f32, kind="Internal").ap()
        PS = [ctx.enter_context(nc.psum_tensor(f"pair{i}", [P, 1024], f32)) for i in range(PAIRS)]

        x_loaded, c_loaded, const_loaded = sem("x_loaded"), sem("c_loaded"), sem("const_loaded")
        raw_loaded = [sem(f"raw_loaded{i}") for i in range(RAW_SLOTS)]
        ada_loaded = [sem(f"ada_loaded{i}") for i in range(ADA_SLOTS)]
        hi_split, lo_split, ada_used = sem("hi_split"), sem("lo_split"), sem("ada_used")
        product_done = sem("product_done")
        sc_ready, eps_set = sem("sc_ready"), sem("eps_set")
        ada_evacuated, mod_ready = sem("ada_evacuated"), sem("mod_ready")
        squared, sq_summed, std_ready, rstd_ready = sem("squared"), sem("sq_summed"), sem("std_ready"), sem("rstd_ready")
        normed, u_hi, u_lo = sem("normed"), sem("u_hi"), sem("u_lo")
        silu_done, glu_done, a_hi, a_lo = sem("silu_done"), sem("glu_done"), sem("a_hi"), sem("a_lo")
        h_updated = sem("h_updated")
        (conv_centre, conv_tap, convolved, staged, l2_squared, l2_std, l2_inv, l2_done, ab_read, gate_chain, gates_ready,
         cum_read, cum_scaled) = (sem(n) for n in
            "conv_centre conv_tap convolved staged l2_squared l2_std l2_inv l2_done ab_read gate_chain gates_ready cum_read cum_scaled".split())
        (dif_done, decay_ready, em_ready, eq_ready, lmat_done, a_ready, at_ready, qk_ready, x1_ready, y1_ready, n_ready, y_ready,
         x_ready, vb_ready, kd_ready, r_ready, qs_ready, vn_ready, s_ready, o_part, o_ready) = (sem("dn_" + n) for n in
            "dif_done decay_ready em_ready eq_ready lmat_done a_ready at_ready qk_ready x1_ready y1_ready n_ready y_ready x_ready vb_ready kd_ready r_ready qs_ready vn_ready s_ready o_part o_ready".split())
        (o_squared, o_summed, o_std, o_inv, o_normed, z_loaded0, z_loaded1, dny_read, dny_hi, dny_lo) = (sem("dn_" + n) for n in
            "o_squared o_summed o_std o_inv o_normed z_loaded0 z_loaded1 y_read y_hi y_lo".split())
        z_loaded = [z_loaded0, z_loaded1]
        masks_loaded, table_made, bias_made, na_loaded, m8_loaded, rope_loaded = (sem(n) for n in
            "masks_loaded table_made bias_made na_loaded m8_loaded rope_loaded".split())
        bias_loaded = [sem(f"bias_loaded{i}") for i in range(2)]
        (bias_scaled, bias_ready, max_done, neg_max, exp_done, sink_done, pt_act, pt_dve, den_done, inv_done, o_read, y_hi, y_lo,
         v_read, odd_read, rope_mul, rope_done) = (sem("at_" + n) for n in
            "bias_scaled bias_ready max_done neg_max exp_done sink_done pt_act pt_dve den_done inv_done o_read y_hi y_lo v_read odd_read rope_mul rope_done".split())
        sink_neg, v_gathered, abs_done = sem("sink_neg"), sem("v_gathered"), sem("dn_abs_done")
        spilled_by = [sem(f"spilled_by{i}") for i in range(2)]
        out_ready, out_stored = sem("out_ready"), [sem(f"out_stored{i}") for i in range(2)]

        def group(x):
            return 2 * x[1] + x[2]

        def released(x):
            kind = x[0]
            n = no[kind][x] + 1
            if kind == "proj":
                if x in conv_no:
                    return [(conv_tap, 4 * conv_no[x] + 4)]
                if x in stage_no:
                    return [(staged, stage_no[x] + 1)]
                return [(ab_read, 1)] if x[2] == "ab" else [(odd_read, odd_no[x] + 1)]
            if kind in RESIDUAL:
                return [(h_updated, res_no[x] + 1)]
            if kind == "dnK":
                return [(r_ready, group(x) - 1), (qs_ready, group(x) - 1)]
            if kind == "PT":
                return [(pt_dve if x[2] else pt_act, x[1] + 1)]
            if kind == "dnT":
                return [(at_ready, n), (qk_ready, n)]
            return [({"ada": ada_evacuated, "norm": std_ready, "gate": silu_done, "up": glu_done, "l2": l2_std,
                      "cum": cum_read, "dnA": lmat_done, "dnN": n_ready, "dnY": y_ready, "dnX": x_ready, "dnV": kd_ready,
                      "dnU": vn_ready, "dnO": o_ready, "dny": dny_read, "vt": v_read, "rope": rope_done, "S": exp_done,
                      "O": o_read, "Y": y_lo}[kind], n)]

        def segs_of(x):
            if x[0] in ("gate", "up", "down"):
                return segments(x[1], x[2])
            if x[0] == "norm":
                return [LAT] if x[1] >= 5 else [LAT, CTX]
            return [LAT] if x[:2] == ("out", 1) or x[:3] == ("proj", 1, "q") else [LAT, CTX]

        def x_before(*match):
            at = next(i for i, x in enumerate(items) if x[:len(match)] == match)
            return [y for y in items[:at] if y[0] in RESIDUAL][-1]

        CONSTS = 16 * 8

        def gate_term(x):
            return 5 if x[0] == "out" else 3 * (2 * x[2]) + 2

        def u_source(x):
            return norm_no[[y for y in norm_items if number[y] < number[x]][-1]]

        def attention(u, a_):
            half = slice(HD * a_, HD * a_ + HD)
            if u < 16:
                jb, i = divmod(u, 4)
                c0 = [0, 8, 24, 32][jb]
                grid = lambda w: nqkv[half, w, i, 0:T_LAT].rearrange("p (r c) -> p r c", c=GRID_W)
                q = nqkv[half, 0, i, P * jb:P * jb + P]
                keys = [(0, 2 * P, grid(1)[:, :, c0:c0 + 32], bias[u % 2][:, a_, :]),
                        (2 * P, 2 * P, nqkv[half, 1, i, T_LAT:T], None)]
                f = slice(P * i + HD * a_, P * i + HD * a_ + HD)
                return q, keys, [vblk[:, 0, f], vblk[:, 1, f], vctx[:, 0, f], vctx[:, 1, f]]
            if u < 24:
                qb, i = divmod(u - 16, 4)
                f = slice(P * i + HD * a_, P * i + HD * a_ + HD)
                return (nqkv[half, 0, i, T_LAT + P * qb:T_LAT + P * qb + P], [(0, 2 * P, nqkv[half, 1, i, T_LAT:T], None)],
                        [vctx[:, 0, f], vctx[:, 1, f]])
            n, t = divmod(u - 24, KD)
            tiles = [m for m in (n - 1, n, n + 1) if 0 <= m < 4] + [4, 5]
            side = {n - 1: wmask[:, 0, :], n + 1: wmask[:, 1, :]}
            keys = [(P * j, P, sw_k[half, t // 4, P * m:P * m + P], side.get(m) if m < 4 else None) for j, m in enumerate(tiles)]
            f = slice(P * (t // 4) + HD * a_, P * (t // 4) + HD * a_ + HD)
            return sq_q[half, t, P * n:P * n + P], keys, [sw_vt[:, m, f] for m in tiles]

        def width(u):
            return P * len(attention(u, 0)[2])

        def prob(u, a_):
            return (prob_e if u < 24 else prob_o)[2 * (u % 2) + a_]

        def probT(u, a_):
            return (probT_e if u < 24 else probT_o)[a_]

        def otok(b):
            return (otok_e if b < 6 else otok_o)[b % 2]

        def tile_of(u):
            return u % 4 if u < 24 else (u - 24) % KD

        def y_target(t, b):
            if b < 4:
                return t[:, 0:4, 0:T_LAT].rearrange("p k (r c) -> p k r c", c=GRID_W)[:, :, :, 16 * b:16 * b + 16]
            if b < 6:
                return t[:, 0:4, T_LAT + P * (b - 4):T_LAT + P * (b - 4) + P]
            return t[:, :, P * (b - 6):P * (b - 6) + P]

        def y_source(pair, b):
            if b < 4:
                return pair[:, 0:4 * P].rearrange("p (k r c) -> p k r c", k=4, c=16)
            return pair[:, 0:(4 if b < 6 else KD) * P].rearrange("p (k q) -> p k q", q=P)

        def per_head(t, tile, d):
            return t[:, tile, 4 * d:4 * d + 4].unsqueeze(2).to_broadcast([P, 4, P])

        def over_heads(m):
            return masks[:, m, :].unsqueeze(1).to_broadcast([P, 4, P])

        v_cols = lambda f: sq[f // 2][:, 2 * P * (f % 2):2 * P * (f % 2) + 2 * P]
        l2_items = list(no.get("l2", {}))
        rope_items = [x for x in odd_no if x[2] in ("k", "q")]
        rope_no = rope_items.index
        o_part_no = {x: j for j, x in enumerate(
            [x for x in items if x[0] == "dnO" and not (SCAN[1 - x[2]].index(SCAN[x[2]][x[1]]) > x[1])])}
        y_tmp = lambda t: cacc[t % 2][:, 0:4 * P].rearrange("p (k q) -> p k q", q=P)

        def l2_after(x):
            if not l2_items:
                return None
            at = number[x]
            ahead = [j for j, y in enumerate(l2_items) if number[y] == at + 4]
            return ahead[0] if ahead else None

        U, STRICT, LEVEL = [0, 1], [2, 3], [4, 4 + LEVELS]

        def pair4(pair, half):
            return pair[:, 512 * half:512 * half + 512].rearrange("p (h s) -> p h s", s=P)

        block = ctx.enter_context(nc.Block())

        @block.sync
        def _(sp):
            sp.dma_start(h[:, :, :], a["xT"]).then_inc(x_loaded, 16)
            sp.dma_start(sc[:, :, :], a["cT"]).then_inc(c_loaded, 16)
            sp.dma_start(ada_b[:, :, :, :], a["ada_bT"]).then_inc(const_loaded, 16)
            sp.dma_start(norm_g[:, :, :], a["norm_gT"]).then_inc(const_loaded, 16)
            sp.dma_start(mean_w[:, :], a["mean_w"]).then_inc(const_loaded, 16)
            sp.dma_start(ones_w[:, :], a["ones_w"]).then_inc(const_loaded, 16)
            sp.dma_start(ident[:, :], a["ident"]).then_inc(const_loaded, 16)
            sp.dma_start(rows[:, :], a["rows"].to_broadcast([P, 40])).then_inc(const_loaded, 16)
            sp.dma_start(conv_w[:, :, :], a["conv_w"]).then_inc(const_loaded, 16)
            sp.dma_start(dn_w[:, :], a["dn_w"]).then_inc(const_loaded, 16)
            nada = 0
            for c in range(16):
                sp.dma_start(toeplitz[c], a["rpb"][:, :, 15 - c:63 - c]).then_inc(table_made, 16)
            sp.wait_ge(table_made, 16 * 16)
            for o in range(3):
                for r in range(ROWS):
                    for hd in range(NA_HEADS):
                        sp.dma_start(bias_hbm[o, hd, r], toeplitz[:, hd, ROWS - 1 - r:2 * ROWS - 1 - r, 16 - 8 * o:48 - 8 * o]) \
                            .then_inc(bias_made, 16)

            def load_bias(u):
                jb, i = divmod(u, 4)
                sp.dma_start(bias[u % 2][:, :, :], bias_hbm[[0, 1, 1, 2][jb], 2 * i:2 * i + 2]
                             .rearrange("h r c a k -> (r c) h (a k)")).then_inc(bias_loaded[u % 2], 16)

            def wait_ada_used(n):
                if n % KD == KD - 1:
                    sp.wait_ge(product_done, number[ada_order[n // KD]] + 1)
                else:
                    sp.wait_ge(ada_used, (KD - 1) * (n // KD) + n % KD + 1)

            for x in items:
                if x[0] == "ada":
                    for i in range(KD):
                        if nada >= ADA_SLOTS:
                            wait_ada_used(nada - ADA_SLOTS)
                        sp.dma_start(ada_raw[nada % ADA_SLOTS][:, :], a["ada_w"][x[1], x[2] * KD + i]) \
                            .then_inc(ada_loaded[nada % ADA_SLOTS], 16)
                        nada += 1
                elif x in slot_of:
                    n = slot_of[x]
                    _, k, w = slots[n]
                    if n >= RAW_SLOTS:
                        sp.wait_ge(lo_split, n - RAW_SLOTS + 1)
                    src = a["w"][slot_at[n]:slot_at[n + 1]].rearrange("(p c) -> p c", p=P)
                    sp.dma_start(raw[n % RAW_SLOTS][:, 0:k * w], src).then_inc(raw_loaded[n % RAW_SLOTS], 16)
                if x == ("proj", 0, "dq", 0):
                    sp.wait_ge(h_updated, KD * len(PARTS))
                    sp.dma_start(masks[:, :, :], a["masks"]).then_inc(masks_loaded, 16)
                if x[0] == "dny":
                    t = x[1]
                    if t == 0:
                        for half in range(2):
                            sp.wait_ge(spilled_by[half], 16 * 8)
                        sp.wait_ge(l2_done, 8)
                    if t >= 2:
                        sp.wait_ge(dny_read, t - 1)
                    sp.dma_start(zt[t % 2].rearrange("p (k q) -> p k q", q=P),
                                 scratch[0:4, :, P * t:P * t + P].rearrange("k p q -> p k q")).then_inc(z_loaded[t % 2], 16)
                if x[0] == "vt" and x == ("vt", 0, 4):
                    sp.wait_ge(dny_lo, STEPS)
                    for w in range(3):
                        sp.dma_start(nqkv[:, w, :, :], scratch[4 + 4 * w:8 + 4 * w].rearrange("k p t -> p k t")) \
                            .then_inc(na_loaded, 16)
                    sp.dma_start(m8[:, :, :], a["m8"]).then_inc(m8_loaded, 16)
                    sp.wait_ge(bias_made, 16 * 3 * ROWS * NA_HEADS)
                    load_bias(0)
                    load_bias(1)
                if x[0] == "O" and x[1] < 14:
                    sp.wait_ge(product_done, number[("S", x[1], 1)] + 1)
                    load_bias(x[1] + 2)
                if x == ("proj", 1, "k", 0):
                    sp.wait_ge(h_updated, res_no[x_before("proj", 1)] + 1)
                    for dst, src in ((rope_c, "rope_c"), (rope_s, "rope_s"), (rope_p, "rope_p"), (wmask, "wmask")):
                        sp.dma_start(dst[(slice(None),) * len(dst.shape)], a[src]).then_inc(rope_loaded, 16)
            for i in range(KD):
                sp.wait_ge(out_ready, i + 1)
                sp.dma_start(out[i], sq[i % 2][:, 0:T_LAT]).then_inc(out_stored[i % 2], 16)
            for i in range(2):
                sp.wait_ge(out_stored[i], 16 * KD // 2)

        @block.gpsimd
        def _(pool):
            nc.gpsimd.memset(eps[:, :], EPS).then_inc(eps_set, 1)
            done = [0]

            def split_up_to(n_slots):
                while done[0] < min(n_slots, len(slots)):
                    n = done[0]
                    _, k, w = slots[n]
                    pool.wait_ge(hi_split, n + 1)
                    nc.gpsimd.tensor_tensor(wl[n % SPLIT_SLOTS][:, 0:k * w], raw[n % RAW_SLOTS][:, 0:k * w],
                                            wh[n % SPLIT_SLOTS][:, 0:k * w].bitcast(f32), ALU.subtract).then_inc(lo_split, 1)
                    done[0] += 1

            for x in items:
                split_up_to(sum(number[y] <= number[x] + 2 for y, _, _ in slots))
                if x[0] == "dnA":
                    d, n = x[2], group(x)
                    pool.wait_ge(decay_ready, n + 1)
                    if n == 0:
                        pool.wait_ge(masks_loaded, 16)
                    nc.gpsimd.tensor_tensor(dEM[d][:, :, :], dE[d][:, :, :], over_heads(STRICT[d]), ALU.mult).then_inc(em_ready, 1)
                    nc.gpsimd.tensor_tensor(dEQ[d][:, :, :], dE[d][:, :, :], over_heads(U[d]), ALU.mult).then_inc(eq_ready, 1)
                elif x[0] == "dnT":
                    d, n = x[2], group(x)
                    pool.wait_ge(a_ready, n + 1)
                    nc.gpsimd.tensor_tensor(dX[d][:, :, :], dA[d][:, :, :], over_heads(LEVEL[d]), ALU.mult).then_inc(x1_ready, 1)
                    pool.wait_ge(at_ready, n + 1)
                    nc.gpsimd.tensor_tensor(dY[d][:, :, :], dAT[d][:, :, :], over_heads(LEVEL[1 - d]), ALU.mult).then_inc(y1_ready, 1)
                elif x == ("dny", 0):
                    for t in range(STEPS):
                        if t < 2:
                            pool.wait_ge(o_ready, 2 * STEPS)
                            pool.wait_ge(spilled_by[t], 16 * 8)
                        if t >= 2:
                            pool.wait_ge(o_summed, t - 1)
                        nc.gpsimd.tensor_tensor(cacc[t % 2][:, 0:4 * P], o_acc[:, t, :], o_acc[:, t, :], ALU.mult).then_inc(o_squared, 1)
                elif x[0] == "vt" and x[1] == 0 and x[2] < 4:
                    jb = x[2]
                    pool.wait_ge(na_loaded, 48)
                    pool.wait_ge(product_done, number[("vt", 0, jb - 1 if jb else 4)] + 1)
                    c0 = [0, 8, 24, 32][jb]
                    for f in range(4):
                        ins = nc.gpsimd.tensor_copy(v_cols(f).rearrange("p (r c) -> p r c", c=32),
                                                    nqkv[:, 2, f, 0:T_LAT].rearrange("p (r c) -> p r c", c=GRID_W)[:, :, c0:c0 + 32])
                    ins.then_inc(v_gathered, 1)
                elif x[0] == "S" and x[1] < 16 and x[2] == 0:
                    u = x[1]
                    pool.wait_ge(bias_loaded[u % 2], 16 * (u // 2 + 1))
                    if u == 0:
                        pool.wait_ge(m8_loaded, 16)
                    b = bias[u % 2][:, :, :]
                    nc.gpsimd.tensor_scalar(b, b, float(HD) ** 0.5, None, ALU.mult).then_inc(bias_scaled, 1)
                    pool.wait_ge(bias_scaled, u + 1)
                    nc.gpsimd.tensor_tensor(b, b, m8[:, [0, 1, 1, 2][u // 4], :].unsqueeze(1).to_broadcast([P, 2, 2 * P]),
                                            ALU.add).then_inc(bias_ready, 1)

        @block.scalar
        def _(act):
            done = [0]

            def split_up_to(n_slots):
                while done[0] < min(n_slots, len(slots)):
                    n = done[0]
                    _, k, w = slots[n]
                    act.wait_ge(raw_loaded[n % RAW_SLOTS], 16 * (n // RAW_SLOTS + 1))
                    if n >= SPLIT_SLOTS:
                        act.wait_ge(product_done, number[slots[n - SPLIT_SLOTS][0]] + 1)
                    nc.scalar.activation(wh[n % SPLIT_SLOTS][:, 0:k * w], raw[n % RAW_SLOTS][:, 0:k * w],
                                         ACT.Copy).then_inc(hi_split, 1)
                    done[0] += 1

            def square(m, i):
                k = KD * m + i
                if k >= 2:
                    act.wait_ge(sq_summed, k - 1)
                nc.scalar.activation(sq[i % 2][:, :], h[:, i, :], ACT.Square).then_inc(squared, 1)

            act.wait_ge(c_loaded, 16)
            nc.scalar.activation(ada_tmp[:, :, :], sc[:, :, :], ACT.Sigmoid).then_inc(sc_ready, 1)
            act.wait_ge(x_loaded, 16)
            act.wait_ge(eps_set, 1)
            for i in range(KD):
                square(0, i)
            for x in items:
                i = number[x]
                split_up_to(sum(number[y] <= i + 2 for y, _, _ in slots))
                if x[0] == "norm":
                    m = norm_no[x]
                    last = segs_of(x)[-1][1]
                    act.wait_ge(product_done, i + 1)
                    if m:
                        act.wait_ge(rstd_ready, m)
                    nc.scalar.activation(std[:, 0:last], PS[i % PAIRS][:, 0:last], ACT.Sqrt,
                                         bias=eps[:, :]).then_inc(std_ready, 1)
                    if x != final:
                        layer, s = x[1] // 3, x[1] % 3
                        for k in range(KD):
                            act.wait_ge(normed, KD * m + k + 1)
                            for v, (lo, hi) in enumerate(segs_of(x)):
                                ins = nc.scalar.activation(uh[:, k, lo:hi], sq[k % 2][:, lo:hi], ACT.Identity,
                                                           bias=mod[:, layer, 3 * s, k, v:v + 1])
                            ins.then_inc(u_hi, 1)
                elif x[0] == "gate":
                    g = glu_no[x[1:]]
                    last = segs_of(x)[-1][1]
                    act.wait_ge(product_done, i + 1)
                    if g >= 2:
                        act.wait_ge(glu_done, g - 1)
                    nc.scalar.activation(sg[g % 2][:, 0:last], PS[i % PAIRS][:, 0:last], ACT.Silu).then_inc(silu_done, 1)
                elif x[0] == "up":
                    g, c = glu_no[x[1:]], x[4]
                    last = segs_of(x)[-1][1]
                    act.wait_ge(glu_done, g + 1)
                    nc.scalar.activation(ah[:, c, 0:last], af[g % 2][:, 0:last], ACT.Copy).then_inc(a_hi, 1)
                elif x in conv_no:
                    c = conv_no[x]
                    act.wait_ge(product_done, i + 1)
                    if c == 0:
                        act.wait_ge(const_loaded, CONSTS)
                    if c >= 2:
                        act.wait_ge(convolved, c - 1)
                    nc.scalar.activation(cacc[c % 2][:, :], PS[i % PAIRS][:, 0:T], ACT.Copy,
                                         scale=conv_w[:, c, 2:3]).then_inc(conv_centre, 1)
                    act.wait_ge(conv_tap, 4 * c + 4)
                    nc.scalar.activation(dqkv[:, c // 4, c % 4, :], cacc[c % 2][:, :], ACT.Silu).then_inc(convolved, 1)
                elif x in stage_no:
                    c = stage_no[x]
                    act.wait_ge(product_done, i + 1)
                    if c == 0:
                        act.wait_ge(convolved, 12)
                    if c >= 2:
                        act.wait_ge(spilled_by[c % 2], 16 * (c // 2))
                    if x[2] == "nq":
                        for jb in range(4):
                            nc.scalar.activation(cacc[c % 2][:, P * jb:P * jb + P].rearrange("p (r c) -> p r c", c=16),
                                                 PS[i % PAIRS][:, 0:T_LAT].rearrange("p (r c) -> p r c", c=GRID_W)
                                                 [:, :, 16 * jb:16 * jb + 16], ACT.Copy)
                        nc.scalar.activation(cacc[c % 2][:, T_LAT:T], PS[i % PAIRS][:, T_LAT:T], ACT.Copy).then_inc(staged, 1)
                    else:
                        nc.scalar.activation(cacc[c % 2][:, :], PS[i % PAIRS][:, 0:T], ACT.Silu if x[2] == "z" else ACT.Copy) \
                            .then_inc(staged, 1)
                    act.wait_ge(staged, c + 1)
                    act.dma_start(scratch[c], cacc[c % 2][:, :]).then_inc(spilled_by[c % 2], 16)
                elif x[0] == "l2":
                    j = no["l2"][x]
                    act.wait_ge(product_done, i + 1)
                    if j:
                        act.wait_ge(l2_inv, j)
                    nc.scalar.activation(std[:, :], PS[i % PAIRS][:, 0:T], ACT.Sqrt, bias=eps[:, :]).then_inc(l2_std, 1)
                elif x[0] == "cum":
                    act.wait_ge(ab_read, 1)
                    nc.scalar.activation(sp_a[:, :, :], ab[:, :, 0:8], ACT.Abs).then_inc(gate_chain, 1)
                    act.wait_ge(gate_chain, 1)
                    nc.scalar.activation(sp_e[:, :, :], sp_a[:, :, :], ACT.Exp, scale=-1.0).then_inc(gate_chain, 1)
                    act.wait_ge(gate_chain, 2)
                    nc.scalar.activation(sp_a[:, :, :], sp_e[:, :, :], ACT.Ln, bias=1.0).then_inc(gate_chain, 1)
                    nc.scalar.activation(ea[:, :], rows[:, 0:8], ACT.Exp).then_inc(gate_chain, 1)
                    nc.scalar.activation(beta[:, :, :], ab[:, :, 8:16], ACT.Sigmoid).then_inc(gate_chain, 1)
                    act.wait_ge(product_done, i + 1)
                    nc.scalar.activation(eg[:, :, :], PS[i % PAIRS][:, 0:48].rearrange("p (t c) -> p t c", c=8), ACT.Exp)
                    nc.scalar.activation(egl[:, :, :], PS[i % PAIRS][:, 48:96].rearrange("p (t c) -> p t c", c=8),
                                         ACT.Exp).then_inc(cum_read, 1)
                    act.wait_ge(cum_scaled, 2)
                    nc.scalar.activation(kdec[:, :, :], kdec[:, :, :], ACT.Exp).then_inc(cum_scaled, 1)
                elif x[0] == "dnA":
                    d, n = x[2], group(x)
                    act.wait_ge(dif_done, n + 1)
                    nc.scalar.activation(dE[d][:, :, :], dE[d][:, :, :], ACT.Abs).then_inc(abs_done, 1)
                    act.wait_ge(abs_done, n + 1)
                    nc.scalar.activation(dE[d][:, :, :], dE[d][:, :, :], ACT.Exp, scale=-1.0).then_inc(decay_ready, 1)
                elif x[0] == "dnT":
                    act.wait_ge(product_done, i + 1)
                    nc.scalar.activation(dAT[x[2]][:, :, :], pair4(PS[i % PAIRS], 0), ACT.Copy).then_inc(at_ready, 1)
                elif x[0] == "dnY":
                    act.wait_ge(product_done, i + 1)
                    nc.scalar.activation(dY[x[2]][:, :, :], pair4(PS[i % PAIRS], 0), ACT.Copy).then_inc(y_ready, 1)
                elif x[0] == "dnK":
                    d, tile = x[2], SCAN[x[2]][x[1]]
                    act.wait_ge(product_done, i + 1)
                    act.wait_ge(lmat_done, group(x) + 1)
                    for hd in range(4):
                        ins = nc.scalar.activation(dQS[d][:, hd, :], pair4(PS[i % PAIRS], 1)[:, hd, :], ACT.Copy,
                                                   scale=eg[:, tile, 4 * d + hd:4 * d + hd + 1])
                    ins.then_inc(qs_ready, 1)
                elif x[0] == "dnU":
                    act.wait_ge(product_done, i + 1)
                    act.wait_ge(qk_ready, group(x) + 1)
                    nc.scalar.activation(dVn[x[2]][:, :, :], pair4(PS[i % PAIRS], 0), ACT.Copy).then_inc(vn_ready, 1)
                elif x[0] == "dny":
                    t = x[1]
                    if t == 0:
                        act.wait_ge(o_summed, STEPS)
                        nc.scalar.activation(oss[:, :, :], oss[:, :, :], ACT.Sqrt, bias=eps[:, :], scale=1.0 / P).then_inc(o_std, 1)
                    act.wait_ge(dny_read, t + 1)
                    nc.scalar.activation(uh[:, 4:8, P * t:P * t + P], y_tmp(t), ACT.Copy).then_inc(dny_hi, 1)
                elif x[0] == "vt":
                    act.wait_ge(product_done, i + 1)
                    if x[1] == 0:
                        dst = vctx if x[2] == 4 else vblk
                        nc.scalar.activation(dst[:, :, :].rearrange("p c f -> p (c f)"), PS[i % PAIRS][:, :], ACT.Copy).then_inc(v_read, 1)
                    else:
                        nc.scalar.activation(sw_vt[:, 3 * x[2]:3 * x[2] + 3, :].rearrange("p c f -> p (c f)"),
                                             PS[i % PAIRS][:, 0:6 * P], ACT.Copy).then_inc(v_read, 1)
                elif x in odd_no:
                    c = odd_no[x]
                    act.wait_ge(product_done, i + 1)
                    if x[2] == "v":
                        nc.scalar.activation(sw_v[:, x[3], :], PS[i % PAIRS][:, 0:T], ACT.Copy).then_inc(odd_read, 1)
                    else:
                        r = rope_no(x)
                        if r >= 2:
                            act.wait_ge(rope_done, r - 1)
                        if x[2] == "k":
                            nc.scalar.activation(sw_k[:, x[3], T_LAT:T], PS[i % PAIRS][:, T_LAT:T], ACT.Copy)
                        nc.scalar.activation(rope_x[r % 2][:, :], PS[i % PAIRS][:, 0:T_LAT], ACT.Copy).then_inc(odd_read, 1)
                elif x[0] == "S":
                    u, a_ = x[1], x[2]
                    w = width(u)
                    act.wait_ge(neg_max, 2 * u + a_ + 1)
                    if u >= 2:
                        act.wait_ge(product_done, number[("PT", u - 2, a_)] + 1)
                    nc.scalar.activation(prob(u, a_)[:, 0:w], PS[i % PAIRS][:, 0:w], ACT.Exp, bias=snb[:, u, a_:a_ + 1],
                                         scale=float(HD) ** -0.5, accum_out=sden[:, u, a_:a_ + 1]).then_inc(exp_done, 1)
                    if u >= 24:
                        col = 24 + 2 * tile_of(u) + a_
                        nc.scalar.activation(ses[:, u, a_:a_ + 1], rows[:, col:col + 1], ACT.Exp,
                                             bias=snb[:, u, a_:a_ + 1]).then_inc(sink_done, 1)
                elif x[0] == "PT" and x[2] == 0:
                    u = x[1]
                    act.wait_ge(product_done, i + 1)
                    if u >= 1:
                        act.wait_ge(product_done, number[("O", u - 1)] + 1)
                    nc.scalar.activation(probT(u, 0)[:, 0:width(u)], PS[i % PAIRS][:, 0:width(u)], ACT.Copy).then_inc(pt_act, 1)
                elif x[0] == "Y":
                    b = x[1]
                    act.wait_ge(product_done, i + 1)
                    for k in range(4 if b < 6 else KD):
                        ins = nc.scalar.activation(y_target(uh, b)[:, k], y_source(PS[i % PAIRS], b)[:, k], ACT.Copy)
                    ins.then_inc(y_hi, 1)
                if x[0] in ("proj", "l2") and l2_after(x) is not None:
                    j = l2_after(x)
                    act.wait_ge(convolved, 12)
                    if j >= 2:
                        act.wait_ge(product_done, number[l2_items[j - 2]] + 1)
                    nc.scalar.activation(sq[j % 2][:, :], dqkv[:, j // 4, j % 4, :], ACT.Square).then_inc(l2_squared, 1)
                if x in squares:
                    act.wait_ge(h_updated, res_no[x] + 1)
                    square(*squares[x])

        @block.vector
        def _(dve):
            dve.wait_ge(sc_ready, 1)
            nc.vector.tensor_tensor(sc[:, :, :], sc[:, :, :], ada_tmp[:, :, :], ALU.mult).then_inc(sc_ready, 1)
            dve.wait_ge(const_loaded, CONSTS)

            def add_square(m, i):
                k = KD * m + i
                dve.wait_ge(squared, k + 1)
                if i == 0:
                    nc.vector.tensor_copy(sumsq[:, :], sq[0][:, :]).then_inc(sq_summed, 1)
                else:
                    dve.wait_ge(sq_summed, k)
                    nc.vector.tensor_tensor(sumsq[:, :], sumsq[:, :], sq[i % 2][:, :], ALU.add).then_inc(sq_summed, 1)

            def low_part(m, k, x):
                layer, s = x[1] // 3, x[1] % 3
                dve.wait_ge(u_hi, KD * m + k + 1)
                for v, (lo, hi) in enumerate(segs_of(x)):
                    ins = nc.vector.scalar_tensor_tensor(out=ul[:, k, lo:hi], in0=sq[k % 2][:, lo:hi],
                                                         scalar=mod[:, layer, 3 * s, k, v:v + 1],
                                                         in1=uh[:, k, lo:hi].bitcast(f32), op0=ALU.add, op1=ALU.subtract)
                ins.then_inc(u_lo, 1)

            for i in range(KD):
                add_square(0, i)
            for x in items:
                i = number[x]
                if x[0] == "ada":
                    n, t = ada_no[x], x[2]
                    dve.wait_ge(product_done, i + 1)
                    if n:
                        dve.wait_ge(mod_ready, n)
                    nc.vector.tensor_tensor(ada_tmp[:, :, :], PS[i % PAIRS][:, 0:2 * KD].rearrange("p (k v) -> p k v", v=2),
                                            ada_b[:, x[1], t, :].unsqueeze(2).to_broadcast([P, KD, 2]),
                                            ALU.add).then_inc(ada_evacuated, 1)
                    dve.wait_ge(ada_evacuated, n + 1)
                    dst = mod[:, x[1], t, :, :]
                    if t % 3 == 0:
                        nc.vector.tensor_copy(dst, ada_tmp[:, :, :]).then_inc(mod_ready, 1)
                    elif t % 3 == 1:
                        g = norm_g[:, 3 * x[1] + t // 3, :].unsqueeze(2).to_broadcast([P, KD, 2])
                        nc.vector.scalar_tensor_tensor(out=dst, in0=ada_tmp[:, :, :], scalar=1.0, in1=g,
                                                       op0=ALU.add, op1=ALU.mult).then_inc(mod_ready, 1)
                    else:
                        nc.vector.tensor_scalar(dst, ada_tmp[:, :, :], 1.0 if t == 5 else 0.5, None,
                                                ALU.mult).then_inc(mod_ready, 1)
                elif x[0] == "norm":
                    m = norm_no[x]
                    last = segs_of(x)[-1][1]
                    layer, s = x[1] // 3, x[1] % 3
                    dve.wait_ge(std_ready, m + 1)
                    nc.vector.reciprocal(rstd[:, 0:last], std[:, 0:last]).then_inc(rstd_ready, 1)
                    dve.wait_ge(rstd_ready, m + 1)
                    if x != final:
                        dve.wait_ge(mod_ready, max(ada_no[("ada", layer, 3 * s)], ada_no[("ada", layer, 3 * s + 1)]) + 1)
                    for k in range(KD):
                        if x == final:
                            if k >= 2:
                                dve.wait_ge(out_stored[k % 2], 16 * (k // 2))
                            nc.vector.scalar_tensor_tensor(out=sq[k % 2][:, 0:last], in0=h[:, k, 0:last],
                                                           scalar=norm_g[:, 3 * DEPTH, k:k + 1], in1=rstd[:, 0:last],
                                                           op0=ALU.mult, op1=ALU.mult).then_inc(out_ready, 1)
                            continue
                        if k >= 2:
                            dve.wait_ge(u_lo, KD * m + k - 1)
                        for v, (lo, hi) in enumerate(segs_of(x)):
                            ins = nc.vector.scalar_tensor_tensor(out=sq[k % 2][:, lo:hi], in0=h[:, k, lo:hi],
                                                                 scalar=mod[:, layer, 3 * s + 1, k, v:v + 1],
                                                                 in1=rstd[:, lo:hi], op0=ALU.mult, op1=ALU.mult)
                        ins.then_inc(normed, 1)
                        if k:
                            low_part(m, k - 1, x)
                    if x != final:
                        low_part(m, KD - 1, x)
                elif x[0] == "up":
                    g, c = glu_no[x[1:]], x[4]
                    last = segs_of(x)[-1][1]
                    dve.wait_ge(product_done, i + 1)
                    dve.wait_ge(silu_done, g + 1)
                    if g >= 2:
                        dve.wait_ge(a_lo, g - 1)
                    nc.vector.tensor_tensor(af[g % 2][:, 0:last], sg[g % 2][:, 0:last], PS[i % PAIRS][:, 0:last],
                                            ALU.mult).then_inc(glu_done, 1)
                    dve.wait_ge(a_hi, g + 1)
                    nc.vector.tensor_tensor(al[:, c, 0:last], af[g % 2][:, 0:last], ah[:, c, 0:last].bitcast(f32),
                                            ALU.subtract).then_inc(a_lo, 1)
                elif x in conv_no:
                    c = conv_no[x]
                    dve.wait_ge(conv_centre, c + 1)
                    for n, j in enumerate((0, 1, 3, 4)):
                        sh = j - 2
                        if n:
                            dve.wait_ge(conv_tap, 4 * c + n)
                        for lo, hi in (LAT, CTX):
                            dst = (lo - min(sh, 0), hi - max(sh, 0))
                            acc = cacc[c % 2][:, dst[0]:dst[1]]
                            ins = nc.vector.scalar_tensor_tensor(out=acc, in0=PS[i % PAIRS][:, dst[0] + sh:dst[1] + sh],
                                                                 scalar=conv_w[:, c, j:j + 1], in1=acc, op0=ALU.mult, op1=ALU.add)
                        ins.then_inc(conv_tap, 1)
                elif x[0] == "proj" and x[2] == "ab":
                    dve.wait_ge(product_done, i + 1)
                    nc.vector.tensor_tensor(ab[:, :, :], PS[i % PAIRS][:, 0:96].rearrange("p (t c) -> p t c", c=16),
                                            rows[:, 8:24].unsqueeze(1).to_broadcast([P, STEPS, 16]), ALU.add).then_inc(ab_read, 1)
                elif x[0] == "l2":
                    j = no["l2"][x]
                    dve.wait_ge(l2_std, j + 1)
                    if j:
                        dve.wait_ge(l2_done, j)
                    nc.vector.reciprocal(rstd[:, :], std[:, :]).then_inc(l2_inv, 1)
                    dve.wait_ge(l2_inv, j + 1)
                    qk = dqkv[:, j // 4, j % 4, :]
                    nc.vector.scalar_tensor_tensor(out=qk, in0=rstd[:, :], scalar=float(P) ** -0.5 if j < 4 else 1.0, in1=qk,
                                                   op0=ALU.mult, op1=ALU.mult).then_inc(l2_done, 1)
                elif x[0] == "cum":
                    dve.wait_ge(gate_chain, 5)
                    nc.vector.scalar_tensor_tensor(out=decay[:, :, :], in0=ab[:, :, 0:8], scalar=0.0, in1=sp_a[:, :, :],
                                                   op0=ALU.max, op1=ALU.add).then_inc(gate_chain, 1)
                    dve.wait_ge(gate_chain, 6)
                    nc.vector.scalar_tensor_tensor(out=decay[:, :, :], in0=decay[:, :, :], scalar=-1.0,
                                                   in1=ea[:, :].unsqueeze(1).to_broadcast([P, STEPS, 8]),
                                                   op0=ALU.mult, op1=ALU.mult).then_inc(gates_ready, 1)
                    dve.wait_ge(cum_read, 1)
                    cols = lambda b: PS[i % PAIRS][:, b:b + 48].rearrange("p (t c) -> p t c", c=8)
                    nc.vector.tensor_copy(gc[:, :, :], cols(0)).then_inc(cum_scaled, 1)
                    dve.wait_ge(cum_scaled, 1)
                    nc.vector.tensor_tensor(kdec[:, :, :], cols(48), gc[:, :, :], ALU.subtract).then_inc(cum_scaled, 1)
                    nc.vector.scalar_tensor_tensor(out=nbe[:, :, :], in0=beta[:, :, :], scalar=-1.0, in1=eg[:, :, :],
                                                   op0=ALU.mult, op1=ALU.mult).then_inc(cum_read, 1)
                elif x[0] == "dnA":
                    d, n, tile = x[2], group(x), SCAN[x[2]][x[1]]
                    dve.wait_ge(product_done, i + 1)
                    nc.vector.tensor_tensor(dE[d][:, :, :], pair4(PS[i % PAIRS], 0), per_head(gc, tile, d),
                                            ALU.subtract).then_inc(dif_done, 1)
                    dve.wait_ge(em_ready, n + 1)
                    for hd in range(4):
                        ins = nc.vector.scalar_tensor_tensor(out=dA[d][:, hd, :], in0=pair4(PS[i % PAIRS], 1)[:, hd, :],
                                                             scalar=beta[:, tile, 4 * d + hd:4 * d + hd + 1],
                                                             in1=dEM[d][:, hd, :], op0=ALU.mult, op1=ALU.mult)
                    ins.then_inc(lmat_done, 1)
                    dve.wait_ge(lmat_done, n + 1)
                    nc.vector.tensor_tensor(dA[d][:, :, :], dA[d][:, :, :], ident[:, :].unsqueeze(1).to_broadcast([P, 4, P]),
                                            ALU.add).then_inc(a_ready, 1)
                elif x[0] == "dnT":
                    d, n = x[2], group(x)
                    dve.wait_ge(product_done, i + 1)
                    dve.wait_ge(eq_ready, n + 1)
                    nc.vector.tensor_tensor(dQK[d][:, :, :], pair4(PS[i % PAIRS], 1), dEQ[d][:, :, :], ALU.mult).then_inc(qk_ready, 1)
                elif x[0] == "dnN":
                    d, k = x[2], x[3]
                    dve.wait_ge(product_done, i + 1)
                    nc.vector.tensor_tensor(dN[d][:, :, :], pair4(PS[i % PAIRS], 0), over_heads(LEVEL[d] + k), ALU.mult).then_inc(n_ready, 1)
                elif x[0] == "dnX":
                    dve.wait_ge(product_done, i + 1)
                    nc.vector.tensor_copy(dX[x[2]][:, :, :], pair4(PS[i % PAIRS], 0)).then_inc(x_ready, 1)
                elif x[0] == "dnV":
                    d, tile = x[2], SCAN[x[2]][x[1]]
                    dve.wait_ge(product_done, i + 1)
                    nc.vector.tensor_tensor(dVb[d][:, :, :], pair4(PS[i % PAIRS], 0), per_head(beta, tile, d), ALU.mult).then_inc(vb_ready, 1)
                    dve.wait_ge(cum_scaled, 3)
                    nc.vector.tensor_tensor(dKd[d][:, :, :], pair4(PS[i % PAIRS], 1), per_head(kdec, tile, d), ALU.mult).then_inc(kd_ready, 1)
                elif x[0] == "dnK":
                    d, tile, n = x[2], SCAN[x[2]][x[1]], group(x)
                    dve.wait_ge(product_done, i + 1)
                    dve.wait_ge(vb_ready, n + 1)
                    dve.wait_ge(eq_ready, n + 1)
                    dve.wait_ge(cum_read, 2)
                    for hd in range(4):
                        ins = nc.vector.scalar_tensor_tensor(out=dR[d][:, hd, :], in0=pair4(PS[i % PAIRS], 0)[:, hd, :],
                                                             scalar=nbe[:, tile, 4 * d + hd:4 * d + hd + 1],
                                                             in1=dVb[d][:, hd, :], op0=ALU.mult, op1=ALU.add)
                    ins.then_inc(r_ready, 1)
                elif x[0] == "dnO":
                    d, st, tile, n = x[2], x[1], SCAN[x[2]][x[1]], group(x)
                    oa = o_acc[:, tile, :].rearrange("p (h e) -> p h e", e=P)
                    pair = PS[i % PAIRS]
                    first = SCAN[1 - d].index(tile) > st or (SCAN[1 - d].index(tile) == st and d == 0)
                    dve.wait_ge(product_done, i + 1)
                    if st == 0:
                        nc.vector.tensor_copy(dS[d][:, :, :], pair4(pair, 1)).then_inc(s_ready, 1)
                        nc.vector.tensor_copy(oa, pair4(pair, 0)).then_inc(o_ready, 1)
                        continue
                    dve.wait_ge(s_ready, n)
                    for hd in range(4):
                        s_h = dS[d][:, hd, :]
                        ins = nc.vector.scalar_tensor_tensor(out=s_h, in0=s_h, scalar=egl[:, tile, 4 * d + hd:4 * d + hd + 1],
                                                             in1=pair4(pair, 1)[:, hd, :], op0=ALU.mult, op1=ALU.add)
                    ins.then_inc(s_ready, 1)
                    dve.wait_ge(qs_ready, n - 1)
                    if first:
                        nc.vector.tensor_tensor(oa, pair4(pair, 0), dQS[d][:, :, :], ALU.add).then_inc(o_ready, 1)
                    else:
                        dve.wait_ge(o_ready, n)
                        nc.vector.tensor_tensor(oa, oa, dQS[d][:, :, :], ALU.add).then_inc(o_part, 1)
                        dve.wait_ge(o_part, o_part_no[x] + 1)
                        nc.vector.tensor_tensor(oa, pair4(pair, 0), oa, ALU.add).then_inc(o_ready, 1)
                elif x[0] == "dny":
                    t = x[1]
                    if t == 0:
                        for q in range(STEPS):
                            dve.wait_ge(o_squared, q + 1)
                            nc.vector.reduce_sum(oss[:, q, :], cacc[q % 2][:, 0:4 * P].rearrange("p (h e) -> p h e", e=P),
                                                 axis=mybir.AxisListType.X).then_inc(o_summed, 1)
                        dve.wait_ge(o_std, 1)
                        nc.vector.reciprocal(oss[:, :, :], oss[:, :, :]).then_inc(o_inv, 1)
                        dve.wait_ge(o_inv, 1)
                        for q in range(STEPS):
                            oa = o_acc[:, q, :].rearrange("p (h e) -> p h e", e=P)
                            nc.vector.tensor_tensor(oa, oa, oss[:, q, :].unsqueeze(2).to_broadcast([P, 4, P]),
                                                    ALU.mult).then_inc(o_normed, 1)
                    dve.wait_ge(product_done, i + 1)
                    dve.wait_ge(z_loaded[t % 2], 16 * (t // 2 + 1))
                    if t >= 2:
                        dve.wait_ge(dny_lo, t - 1)
                    nc.vector.scalar_tensor_tensor(out=y_tmp(t), in0=pair4(PS[i % PAIRS], 0), scalar=dn_w[:, :],
                                                   in1=zt[t % 2].rearrange("p (k q) -> p k q", q=P),
                                                   op0=ALU.mult, op1=ALU.mult).then_inc(dny_read, 1)
                    dve.wait_ge(dny_hi, t + 1)
                    nc.vector.tensor_tensor(ul[:, 4:8, P * t:P * t + P], y_tmp(t), uh[:, 4:8, P * t:P * t + P].bitcast(f32),
                                            ALU.subtract).then_inc(dny_lo, 1)
                elif x[0] == "rope":
                    r = x[1]
                    dve.wait_ge(product_done, i + 1)
                    if r == 0:
                        dve.wait_ge(rope_loaded, 64)
                    dst = sw_k[:, r, 0:T_LAT] if r < 2 else sq_q[:, r - 2, :]
                    xr = rope_x[r % 2][:, :]
                    nc.vector.tensor_tensor(dst, PS[i % PAIRS][:, 0:T_LAT], rope_s[:, :], ALU.mult).then_inc(rope_mul, 1)
                    nc.vector.tensor_tensor(xr, xr, rope_c[:, :], ALU.mult).then_inc(rope_mul, 1)
                    dve.wait_ge(rope_mul, 2 * r + 2)
                    nc.vector.tensor_tensor(dst, dst, xr, ALU.add).then_inc(rope_done, 1)
                elif x[0] == "S":
                    u, a_ = x[1], x[2]
                    n = 2 * u + a_
                    dve.wait_ge(product_done, i + 1)
                    nc.vector.reduce_max(smx[:, u, a_:a_ + 1], PS[i % PAIRS][:, 0:width(u)], axis=mybir.AxisListType.X).then_inc(max_done, 1)
                    dve.wait_ge(max_done, n + 1)
                    if u < 24:
                        nc.vector.tensor_scalar(snb[:, u, a_:a_ + 1], smx[:, u, a_:a_ + 1], -float(HD) ** -0.5, None,
                                                ALU.mult).then_inc(neg_max, 1)
                    else:
                        if n == 48:
                            nc.vector.tensor_scalar(nsink[:, :], rows[:, 24:40], -1.0, None, ALU.mult).then_inc(sink_neg, 1)
                            dve.wait_ge(sink_neg, 1)
                        col = 2 * tile_of(u) + a_
                        nc.vector.tensor_scalar(snb[:, u, a_:a_ + 1], smx[:, u, a_:a_ + 1], -float(HD) ** -0.5,
                                                nsink[:, col:col + 1], ALU.mult, ALU.min).then_inc(neg_max, 1)
                elif x[0] == "PT" and x[2] == 1:
                    u = x[1]
                    dve.wait_ge(product_done, i + 1)
                    if u >= 1:
                        dve.wait_ge(product_done, number[("O", u - 1)] + 1)
                    nc.vector.tensor_copy(probT(u, 1)[:, 0:width(u)], PS[i % PAIRS][:, 0:width(u)]).then_inc(pt_dve, 1)
                elif x[0] == "O":
                    u = x[1]
                    b = block_of(u)
                    den = sden[:, u, :]
                    dve.wait_ge(exp_done, 2 * u + 2)
                    if u >= 24:
                        dve.wait_ge(sink_done, 2 * (u - 24) + 2)
                        nc.vector.tensor_tensor(den, den, ses[:, u, :], ALU.add).then_inc(den_done, 1)
                        dve.wait_ge(den_done, u - 23)
                    nc.vector.reciprocal(srec[:, u, :], den).then_inc(inv_done, 1)
                    dve.wait_ge(inv_done, u + 1)
                    dve.wait_ge(product_done, i + 1)
                    if b >= 2 and (u % 4 if u < 24 else (u - 24) % KD) == 0 and ("Y", b - 2) in number:
                        dve.wait_ge(product_done, number[("Y", b - 2)] + 1)
                    nc.vector.tensor_tensor(otok(b)[:, P * tile_of(u):P * tile_of(u) + P].rearrange("p (a e) -> p a e", e=HD),
                                            PS[i % PAIRS][:, 0:P].rearrange("p (a e) -> p a e", e=HD),
                                            srec[:, u, :].unsqueeze(2).to_broadcast([P, 2, HD]), ALU.mult).then_inc(o_read, 1)
                elif x[0] == "Y":
                    b = x[1]
                    dve.wait_ge(y_hi, b + 1)
                    for k in range(4 if b < 6 else KD):
                        ins = nc.vector.tensor_tensor(y_target(ul, b)[:, k], y_source(PS[i % PAIRS], b)[:, k],
                                                      y_target(uh, b)[:, k].bitcast(f32), ALU.subtract)
                    ins.then_inc(y_lo, 1)
                elif x[0] in RESIDUAL:
                    k = x[-1]
                    dve.wait_ge(product_done, i + 1)
                    dve.wait_ge(mod_ready, ada_no[("ada", x[1], gate_term(x))] + 1)
                    if res_no[x] >= KD:
                        dve.wait_ge(h_updated, res_no[x] - KD + 1)
                    for v, (lo, hi) in enumerate(segs_of(x)):
                        ins = nc.vector.scalar_tensor_tensor(out=h[:, k, lo:hi], in0=PS[i % PAIRS][:, lo:hi],
                                                             scalar=mod[:, x[1], gate_term(x), k, v:v + 1],
                                                             in1=h[:, k, lo:hi], op0=ALU.mult, op1=ALU.add)
                    ins.then_inc(h_updated, 1)
                    if x in squares:
                        m, q = squares[x]
                        if q:
                            add_square(m, q - 1)
                        if q == KD - 1:
                            add_square(m, q)

        @block.tensor
        def _(pe):
            waited = [0]
            nada = 0

            def dense(x, pair, xh, xl, ready=None):
                n = slot_of[x]
                _, K, w = slots[n]
                pe.wait_ge(lo_split, n + 1)
                for k in range(K):
                    if ready:
                        ready(k)
                    for wt, xt, first, last in ((wh, xh, k == 0, False), (wh, xl, False, False),
                                                (wl, xh, False, k == K - 1)):
                        for lo, hi in segs_of(x):
                            ins = nc.tensor.matmul(pair[:, lo:hi], wt[n % SPLIT_SLOTS][:, k * P:(k + 1) * P],
                                                   xt[:, k, lo:hi], start=first, stop=last)
                return ins

            pe.wait_ge(sc_ready, 2)
            fresh_norm = [-1]
            for x in items:
                i = number[x]
                pair = PS[i % PAIRS]
                if i >= PAIRS:
                    for signal in released(items[i - PAIRS]):
                        pe.wait_ge(*signal)
                if x[0] == "ada":
                    for t in range(KD):
                        pe.wait_ge(ada_loaded[nada % ADA_SLOTS], 16 * (nada // ADA_SLOTS + 1))
                        for k in range(KD):
                            ins = nc.tensor.matmul(pair[:, 2 * t:2 * t + 2], ada_raw[nada % ADA_SLOTS][:, k * P:(k + 1) * P],
                                                   sc[:, k, :], start=k == 0, stop=k == KD - 1)
                        nada += 1
                        if t < KD - 1:
                            ins.then_inc(ada_used, 1)
                    ins.then_inc(product_done, 1)
                elif x[0] == "norm":
                    pe.wait_ge(sq_summed, KD * (norm_no[x] + 1))
                    pe.wait_ge(const_loaded, CONSTS)
                    for lo, hi in segs_of(x):
                        ins = nc.tensor.matmul(pair[:, lo:hi], mean_w[:, :], sumsq[:, lo:hi], start=True, stop=True)
                    ins.then_inc(product_done, 1)
                elif x[0] == "proj" and x[2] == "ab":
                    n = slot_of[x]
                    pe.wait_ge(lo_split, n + 1)
                    for t in range(STEPS):
                        for k in range(KD):
                            for ut, wt, first, last in ((uh, wh, k == 0, False), (uh, wl, False, False), (ul, wh, False, k == KD - 1)):
                                ins = nc.tensor.matmul(pair[:, 16 * t:16 * t + 16], ut[:, k, P * t:P * t + P],
                                                       wt[n % SPLIT_SLOTS][:, 16 * k:16 * k + 16], start=first, stop=last)
                    ins.then_inc(product_done, 1)
                elif x in slot_of:
                    m = u_source(x)
                    ready = None
                    if x[0] in ("gate", "up", "proj") and fresh_norm[0] != m:
                        fresh_norm[0] = m
                        ready = lambda k: pe.wait_ge(u_lo, KD * m + k + 1)
                    if x[0] == "down" and x[4] == 0:
                        first = glu_no[next(y for y in items if y[0] == "up" and y[1:4] == x[1:4])[1:]]
                        ready = lambda k: pe.wait_ge(a_lo, first + k + 1)
                    if x[0] == "out" and x[2] == 0:
                        pe.wait_ge(y_lo, 6 if x[1] == 0 else 10)
                        pe.wait_ge(dny_lo, STEPS)
                    src = (ah, al) if x[0] == "down" else (uh, ul)
                    dense(x, pair, *src, ready=ready).then_inc(product_done, 1)
                elif x[0] == "l2":
                    j = no["l2"][x]
                    pe.wait_ge(l2_squared, j + 1)
                    for lo, hi in (LAT, CTX):
                        ins = nc.tensor.matmul(pair[:, lo:hi], ones_w[:, :], sq[j % 2][:, lo:hi], start=True, stop=True)
                    ins.then_inc(product_done, 1)
                elif x[0] == "cum":
                    pe.wait_ge(gates_ready, 1)
                    pe.wait_ge(masks_loaded, 16)
                    cols = lambda b: pair[:, b:b + 48].rearrange("p (t c) -> p t c", c=8)
                    for d in range(2):
                        nc.tensor.matmul(cols(0)[:, :, 4 * d:4 * d + 4], masks[:, U[d], :], decay[:, :, 4 * d:4 * d + 4],
                                         start=True, stop=True)
                    nc.tensor.matmul(pair[:, 48:96], ones_w[:, :], decay[:, :, :].rearrange("p t c -> p (t c)"),
                                     start=True, stop=True).then_inc(product_done, 1)
                elif x[0] == "dnA":
                    d, tile = x[2], SCAN[x[2]][x[1]]
                    if x[1] == 0:
                        pe.wait_ge(l2_done, 8)
                        pe.wait_ge(cum_read, 2)
                    kT = dqkv[:, 1, :, P * tile:P * tile + P]
                    for hd in range(4):
                        c = 4 * d + hd
                        nc.tensor.matmul(pair4(pair, 0)[:, hd, :], decay[:, tile, c:c + 1].to_broadcast([P, P]), masks[:, U[d], :],
                                         start=True, stop=True)
                    for hd in range(4):
                        ins = nc.tensor.matmul(pair4(pair, 1)[:, hd, :], kT[:, hd, :], kT[:, hd, :], start=True, stop=True)
                    ins.then_inc(product_done, 1)
                elif x[0] == "dnT":
                    d, tile = x[2], SCAN[x[2]][x[1]]
                    for hd in range(4):
                        nc.tensor.matmul(pair4(pair, 1)[:, hd, :], dqkv[:, 1, hd, P * tile:P * tile + P],
                                         dqkv[:, 0, hd, P * tile:P * tile + P], start=True, stop=True)
                    pe.wait_ge(a_ready, group(x) + 1)
                    for hd in range(4):
                        ins = nc.tensor.transpose(pair4(pair, 0)[:, hd, :], dA[d][:, hd, :], ident[:, :])
                    ins.then_inc(product_done, 1)
                elif x[0] == "dnN":
                    d, k, n = x[2], x[3], group(x)
                    if k == 1:
                        pe.wait_ge(at_ready, n + 1)
                        pe.wait_ge(x1_ready, n + 1)
                    else:
                        pe.wait_ge(x_ready, no["dnX"][("dnX", x[1], d, k - 1)] + 1)
                    for hd in range(4):
                        ins = nc.tensor.matmul(pair4(pair, 0)[:, hd, :], dAT[d][:, hd, :], dX[d][:, hd, :], start=True, stop=True)
                    ins.then_inc(product_done, 1)
                elif x[0] == "dnY":
                    d, k, n = x[2], x[3], group(x)
                    pe.wait_ge(n_ready, no["dnN"][("dnN",) + x[1:]] + 1)
                    if k == 1:
                        pe.wait_ge(y1_ready, n + 1)
                    for hd in range(4):
                        ins = nc.tensor.matmul(pair4(pair, 0)[:, hd, :], dN[d][:, hd, :], dY[d][:, hd, :], start=True, stop=True)
                    ins.then_inc(product_done, 1)
                elif x[0] == "dnX":
                    d = x[2]
                    pe.wait_ge(y_ready, no["dnY"][("dnY",) + x[1:]] + 1)
                    for hd in range(4):
                        ins = nc.tensor.transpose(pair4(pair, 0)[:, hd, :], dY[d][:, hd, :], ident[:, :])
                    ins.then_inc(product_done, 1)
                elif x[0] == "dnV":
                    tile = SCAN[x[2]][x[1]]
                    for w, half in ((2, 0), (1, 1)):
                        for hd in range(4):
                            ins = nc.tensor.transpose(pair4(pair, half)[:, hd, :], dqkv[:, w, hd, P * tile:P * tile + P], ident[:, :])
                    ins.then_inc(product_done, 1)
                elif x[0] == "dnK":
                    d, tile, n = x[2], SCAN[x[2]][x[1]], group(x)
                    pe.wait_ge(s_ready, n - 1)
                    for w, half in ((1, 0), (0, 1)):
                        for hd in range(4):
                            ins = nc.tensor.matmul(pair4(pair, half)[:, hd, :], dqkv[:, w, hd, P * tile:P * tile + P],
                                                   dS[d][:, hd, :], start=True, stop=True)
                    ins.then_inc(product_done, 1)
                elif x[0] == "dnU":
                    d, n = x[2], group(x)
                    if x[1]:
                        pe.wait_ge(r_ready, n - 1)
                    pe.wait_ge(vb_ready, n + 1)
                    pe.wait_ge(y_ready, no["dnY"][("dnY", x[1], d, LEVELS - 1)] + 1)
                    for hd in range(4):
                        ins = nc.tensor.matmul(pair4(pair, 0)[:, hd, :], dY[d][:, hd, :], (dR if x[1] else dVb)[d][:, hd, :],
                                               start=True, stop=True)
                    ins.then_inc(product_done, 1)
                elif x[0] == "dnO":
                    d, n = x[2], group(x)
                    pe.wait_ge(vn_ready, n + 1)
                    pe.wait_ge(qk_ready, n + 1)
                    pe.wait_ge(kd_ready, n + 1)
                    for lhs, half in ((dQK, 0), (dKd, 1)):
                        for hd in range(4):
                            ins = nc.tensor.matmul(pair4(pair, half)[:, hd, :], lhs[d][:, hd, :], dVn[d][:, hd, :],
                                                   start=True, stop=True)
                    ins.then_inc(product_done, 1)
                elif x[0] == "dny":
                    pe.wait_ge(o_normed, x[1] + 1)
                    for hd in range(4):
                        ins = nc.tensor.transpose(pair4(pair, 0)[:, hd, :], o_acc[:, x[1], P * hd:P * hd + P], ident[:, :])
                    ins.then_inc(product_done, 1)
                elif x[0] == "vt":
                    if x == ("vt", 0, 4):
                        pe.wait_ge(na_loaded, 48)
                    if x[1] == 0 and x[2] < 4:
                        pe.wait_ge(v_gathered, x[2] + 1)
                    if x[1] == 0:
                        for c in range(2):
                            for f in range(4):
                                v = nqkv[:, 2, f, :]
                                if x[2] == 4:
                                    src = v[:, T_LAT + P * c:T_LAT + P * c + P]
                                else:
                                    src = v_cols(f)[:, P * c:P * c + P]
                                ins = nc.tensor.transpose(pair[:, 512 * c + P * f:512 * c + P * f + P], src, ident[:, :])
                    else:
                        pe.wait_ge(odd_read, odd_no[("proj", 1, "v", 1)] + 1)
                        for t in range(3):
                            for f in range(2):
                                m = 3 * x[2] + t
                                ins = nc.tensor.transpose(pair[:, 256 * t + P * f:256 * t + P * f + P],
                                                          sw_v[:, f, P * m:P * m + P], ident[:, :])
                    ins.then_inc(product_done, 1)
                elif x[0] == "rope":
                    r = x[1]
                    pe.wait_ge(odd_read, odd_no[rope_items[r]] + 1)
                    pe.wait_ge(rope_loaded, 64)
                    nc.tensor.matmul(pair[:, 0:T_LAT], rope_p[:, :], rope_x[r % 2][:, :], start=True, stop=True) \
                        .then_inc(product_done, 1)
                elif x[0] == "S":
                    u, a_ = x[1], x[2]
                    q, keys, _ = attention(u, a_)
                    if u == 0:
                        pe.wait_ge(na_loaded, 48)
                    if u < 16:
                        pe.wait_ge(bias_ready, u + 1)
                    if u == 24:
                        pe.wait_ge(rope_done, 10)
                    for col, n, k, extra in keys:
                        ins = nc.tensor.matmul(pair[:, col:col + n], q, k, start=True, stop=extra is None)
                        if extra is not None:
                            ins = nc.tensor.matmul(pair[:, col:col + n], ident[:, :], extra, start=False, stop=True)
                    ins.then_inc(product_done, 1)
                elif x[0] == "PT":
                    u, a_ = x[1], x[2]
                    pe.wait_ge(exp_done, 2 * u + a_ + 1)
                    for c in range(width(u) // P):
                        ins = nc.tensor.transpose(pair[:, P * c:P * c + P], prob(u, a_)[:, P * c:P * c + P], ident[:, :])
                    ins.then_inc(product_done, 1)
                elif x[0] == "O":
                    u = x[1]
                    pe.wait_ge(pt_act, u + 1)
                    pe.wait_ge(pt_dve, u + 1)
                    pe.wait_ge(v_read, 7 if u >= 24 else 5 if u >= 12 else u // 4 + 2)
                    for a_ in range(2):
                        vs = attention(u, a_)[2]
                        for c, v in enumerate(vs):
                            ins = nc.tensor.matmul(pair[:, HD * a_:HD * a_ + HD], probT(u, a_)[:, P * c:P * c + P], v,
                                                   start=c == 0, stop=c == len(vs) - 1)
                    ins.then_inc(product_done, 1)
                elif x[0] == "Y":
                    b = x[1]
                    pe.wait_ge(o_read, 4 * b + 4 if b < 6 else 24 + KD * (b - 5))
                    for k in range(4 if b < 6 else KD):
                        ins = nc.tensor.transpose(pair[:, P * k:P * k + P], otok(b)[:, P * k:P * k + P], ident[:, :])
                    ins.then_inc(product_done, 1)


def feature_major(v):
    return v.reshape(-1, P, v.shape[-1]).transpose(1, 0, 2)


def weight_of(x, n, inputs):
    if x[0] in ("gate", "up"):
        w = inputs["ffn_w_up"][x[1], x[2]]
        c = x[5] * P + (D_FF if x[0] == "up" else 0)
        return w[:, c:c + P]
    if x[0] == "down":
        r = sum(PARTS[:x[3]]) * P
        return inputs["ffn_w_down"][x[1], x[2]][r:r + PARTS[x[3]] * P, x[4] * P:(x[4] + 1) * P]
    return mixer_weight(x, inputs)


def query_heads(t):
    per = SWA_HEADS // SWA_KV
    return [(2 * (t // per) + a) * per + t % per for a in range(2)]


def mixer_weight(x, inputs):
    if x[0] == "proj" and x[1] == 0:
        w, i = inputs["even_w_in"][0], x[3]
        first = {"nq": 0, "nk": 512, "nv": 1024, "dq": NA_PROJ, "dk": NA_PROJ + 512, "dv": NA_PROJ + 1024,
                 "z": NA_PROJ + DN_QKV, "ab": NA_PROJ + DN_QKV + DN_HEADS * P}[x[2]]
        return w[:, first + P * i:first + (16 if x[2] == "ab" else P * i + P)]
    if x[0] == "proj":
        w, i = inputs["odd_w_in"][0], x[3]
        if x[2] == "q":
            return np.concatenate([w[:, HD * q:HD * q + HD] for q in query_heads(i)], 1)
        first = SWA_HEADS * HD + (0 if x[2] == "k" else SWA_KV * HD)
        return w[:, first + P * i:first + P * i + P]
    cols = slice(P * x[2], P * x[2] + P)
    if x[1] == 0:
        return inputs["even_w_out"][0][:, cols]
    w = inputs["odd_w_out"][0]
    return np.concatenate([w[HD * q:HD * q + HD, cols] for t in range(KD) for q in query_heads(t)], 0)


def constants():
    i, j = np.arange(P)[:, None], np.arange(P)[None, :]
    f = lambda x: np.asarray(x, np.float32)
    level = lambda b: f(i == j) - f((i // b == j // b + 1) & ((j // b) % 2 == 0))
    lower = [level(2 ** k) for k in range(LEVELS)]
    masks = [f(i <= j), f(i >= j), f(i > j), f(i < j)] + lower + [m.T for m in lower]
    m8 = []
    for jb in (0, 1, 3):
        qc = 16 * jb + np.arange(16)
        kc = min(max(16 * jb - 8, 0), 32) + np.arange(32)
        start = np.clip(qc - 8, 0, 48)[:, None]
        ok = (kc >= start) & (kc < start + 16)
        m8.append(np.tile(np.where(ok, 0.0, NEG * HD ** 0.5), (ROWS, ROWS)))
    wmask = [np.where(j >= i, 0.0, NEG * HD ** 0.5), np.where(j <= i, 0.0, NEG * HD ** 0.5)]
    t = np.arange(T_LAT)
    inv = np.power(np.float32(10000.0), -np.arange(0, 32, 2, dtype=np.float32) / np.float32(32))
    feat = np.arange(P) % HD
    pos = np.where((feat < 32)[:, None], t // GRID_W, t % GRID_W).astype(np.float32)
    ang = pos * inv[feat % 16][:, None]
    sign = np.where(feat % 32 < 16, -1.0, 1.0)[:, None]
    return {
        "masks": f(np.stack(masks, 1)), "m8": f(np.stack(m8, 1)), "wmask": f(np.stack(wmask, 1)),
        "rope_c": f(np.cos(ang)), "rope_s": f(np.sin(ang) * sign), "rope_p": f(j == (i ^ 16)),
        "ident": np.eye(P, dtype=np.float32), "ones_w": np.ones((P, P), np.float32),
        "mean_w": np.full((P, P), 1.0 / D, np.float32),
    }


def layouts(inputs, items):
    x = np.concatenate([inputs["x"][0], inputs["ctx"][0]], 0).T
    cs = np.stack([inputs["c"][0], inputs["c_ctx"]], 1)
    ada = inputs["ada_w"].reshape(DEPTH, KD, P, N_MOD * KD, P).transpose(0, 3, 2, 1, 4)
    gs = np.concatenate([inputs["norm_g"].reshape(DEPTH * 3, D), inputs["final_norm_g"][None]], 0)
    parts = [feature_major(weight_of(y, n, inputs)).reshape(-1) for n, (y, _, _) in enumerate(weight_slots(items))]
    return {
        "xT": feature_major(x),
        "cT": feature_major(cs),
        "ada_w": ada.reshape(DEPTH, N_MOD * KD, P, KD * P),
        "ada_bT": inputs["ada_b"].reshape(DEPTH, N_MOD, KD, P).transpose(3, 0, 1, 2),
        "norm_gT": gs.reshape(-1, KD, P).transpose(2, 0, 1),
        "rows": np.concatenate([inputs["dn_a_log"][0].reshape(-1), inputs["dn_dt_bias"][0].reshape(-1), np.zeros(8, np.float32),
                                np.concatenate([inputs["swa_sink"][0][query_heads(t)] for t in range(KD)])])[None],
        "conv_w": inputs["dn_conv_w"][0].reshape(CONV, 12, P).transpose(2, 1, 0),
        "dn_w": inputs["dn_norm_w"][0][:, None],
        "rpb": np.pad(inputs["na_rpb"][0], ((0, 0), (0, 0), (16, 16))),
        "w": np.concatenate(parts),
        **constants(),
    }


def kernel(**inputs):
    import concourse.bacc as bacc
    from concourse.bass_utils import run_bass_kernel_spmd

    inputs = {k: np.asarray(v) for k, v in inputs.items()}
    items = schedule()
    arrays = {k: np.ascontiguousarray(v) for k, v in layouts(inputs, items).items()}
    nc = bacc.Bacc("TRN2", target_bir_lowering=False, num_devices=1)
    aps = {k: nc.dram_tensor(f"in_{k}", v.shape, mybir.dt.from_np(v.dtype), kind="ExternalInput").ap()
           for k, v in arrays.items()}
    out = nc.dram_tensor("out_h", (KD, P, T_LAT), mybir.dt.float32, kind="ExternalOutput").ap()
    build(nc, aps, out, items)
    r = run_bass_kernel_spmd(nc, [{f"in_{k}": v for k, v in arrays.items()}], core_ids=[0])
    return r.results[0]["out_h"].transpose(2, 0, 1).reshape(1, T_LAT, D)
```

```python
import numpy as np
import concourse.bass as bass
from concourse import mybir
from contextlib import ExitStack

D = 1024
T_LAT, T_CTX = 512, 256
T = T_LAT + T_CTX
P = 128
KD = D // P
DEPTH = 2
N_MOD = 9
D_FF = 2816
FFC = D_FF // P
PARTS = [8, 7, 7]
EPS = 1e-6
LAT, CTX = (0, T_LAT), (T_LAT, T)
NA_HEADS, DN_HEADS, SWA_HEADS, SWA_KV = 8, 4, 16, 4
HD = 64
GRID_W, ROWS = 64, T_LAT // 64
NA_PROJ = 3 * NA_HEADS * HD
DN_QKV = DN_HEADS * 3 * P
CONV = 5

RAW_SLOTS, SPLIT_SLOTS = 4, 3
ADA_SPLIT = 4
ADA_FIRST = 7
NEG = -1e30


def segments(layer, f):
    return [LAT] if (layer, f) == (DEPTH - 1, 1) else [LAT, CTX]


def ffn_products(layer, f):
    items = []
    j = 0
    for part, n in enumerate(PARTS):
        for c in range(n):
            items += [("gate", layer, f, part, c, j), ("up", layer, f, part, c, j)]
            j += 1
        items += [("down", layer, f, part, i) for i in range(KD)]
    return items


def insert_before(items, match, extra):
    at = next(i for i, x in enumerate(items) if x[:len(match)] == match)
    return items[:at] + extra + items[at:]


def ada_products(layer, terms):
    return [("ada", layer, t, q) for t in terms for q in range(ADA_SPLIT)]


def spread(items, extra, first=0, last=None):
    last = len(items) if last is None else last
    at = [first + (last - first) * (i + 1) // (len(extra) + 1) for i in range(len(extra))]
    out = []
    for i, x in enumerate(items + [None]):
        out += [e for e, a in zip(extra, at) if a == i]
        out += [x] if x is not None else []
    return out


def schedule(mixers=True):
    s = ada_products(0, [0, 1]) + [("norm", 0)]
    f = ffn_products(0, 0)
    n = next(i for i, x in enumerate(f) if x[0] == "down")
    s += spread(f[:n], ada_products(0, [2])) + spread(f[n:], ada_products(0, range(3, 9)))
    if mixers:
        s += even_products()
    else:
        s += ada_products(1, range(9))
    s += [("norm", 2)] + ffn_products(0, 1) + [("norm", 3)] + ffn_products(1, 0)
    if mixers:
        s += odd_products()
    s += [("norm", 5)] + ffn_products(1, 1) + [("norm", 6)]
    return s


SCAN = [[4, 5, 0, 1, 2, 3], [5, 4, 3, 2, 1, 0]]
STEPS = T // P
LEVELS = 7


def attention_products(layer, units, values_before):
    items = [("S", u, a) for u in units[:2] for a in range(2)]
    for u in units:
        items += values_before.get(u, []) + [("PT", u)]
        items += [("S", u + 2, a) for a in range(2) if u + 2 <= units[-1]]
        items.append(("O", u))
        if last_of_block(u):
            items.append(("Y", block_of(u)))
    return items


def block_of(u):
    return u // 4 if u < 24 else 6 + (u - 24) // 8


def last_of_block(u):
    return u % 4 == 3 if u < 24 else (u - 24) % 8 == 7


def even_products():
    s = [("norm", 1)]
    s += [("proj", 0, w, i) for w in ("dq", "dk", "dv") for i in range(4)] + [("proj", 0, "ab", 0)]
    s += [("proj", 0, "z", i) for i in range(4)]
    norms = [("l2", w, i) for w in ("dq", "dk") for i in range(4)]
    for i, x in enumerate([("proj", 0, w, i) for w in ("nq", "nk", "nv") for i in range(4)]):
        s += [x] + norms[i:i + 1]
    s += [("cum",)]
    both = lambda kind, *r: [(kind, r[0], d, *r[1:]) for d in range(2)]

    def step(st, scan, mine):
        gaps = [both("dnT", st)]
        for k in range(1, LEVELS):
            gaps += [both("dnN", st, k), both("dnY", st, k)] + ([both("dnX", st, k)] if k < LEVELS - 1 else [])
        out = both("dnA", st) + mine[:1] + scan[:2]
        scan, mine = scan[2:], mine[1:]
        n = len(gaps)
        for i, g in enumerate(gaps):
            out += g
            out += scan[len(scan) * i // 9:len(scan) * (i + 1) // 9] if i < 9 else []
            out += mine[len(mine) * i // n:len(mine) * (i + 1) // n]
        return out

    def merge(scan, mine):
        out = []
        for i in range(max(len(scan), len(mine))):
            out += scan[i:i + 1] + mine[i:i + 1]
        return out

    ada = ada_products(1, range(N_MOD))
    s += step(0, [], ada[:6])
    ada = ada[6:]
    for st in range(STEPS):
        s += both("dnV", st)
        scan = (both("dnK", st) if st else []) + both("dnU", st) + both("dnO", st)
        share = -(-len(ada) // (STEPS - st))
        mine, ada = ada[:share], ada[share:]
        if st < STEPS - 1:
            s += step(st + 1, scan, mine)
        else:
            s += merge(scan, mine)
    s += [("dny", t) for t in range(STEPS)]
    before = {4 * jb: [("vt", 0, jb)] for jb in range(4)}
    before[0] = [("vt", 0, 4)] + before[0]
    s += attention_products(0, list(range(24)), before)
    return s + [("out", 0, i) for i in range(KD)]


def odd_products():
    s = [("norm", 4)]
    order = [("proj", 1, w, i) for w, n in (("k", 2), ("q", 8)) for i in range(n)]
    for i, x in enumerate(order):
        s.append(x)
        if i:
            s.append(("rope", i - 1))
        if i == 1:
            s += [("proj", 1, "v", 0), ("proj", 1, "v", 1)]
    s += [("rope", len(order) - 1), ("vt", 1, 0), ("vt", 1, 1)]
    s += attention_products(1, list(range(24, 56)), {})
    return s + [("out", 1, i) for i in range(KD)]


RESIDUAL = ("down", "out")


def weight_slots(items):
    out = []
    for x in items:
        if x[0] in ("gate", "up", "out", "proj"):
            out.append((x, KD, 16 if x[2] == "ab" else P))
        elif x[0] == "down":
            out.append((x, PARTS[x[3]], P))
    return out


def build(nc, a, out, items):
    f32, f32r = mybir.dt.float32, mybir.dt.float32r
    ALU, ACT = mybir.AluOpType, mybir.ActivationFunctionType

    slots = weight_slots(items)
    slot_of = {x: n for n, (x, _, _) in enumerate(slots)}
    slot_at = np.concatenate([[0], np.cumsum([P * k * w for _, k, w in slots])]).tolist()
    number = {x: i for i, x in enumerate(items)}
    ada_order = [x for x in items if x[0] == "ada"]
    ada_no = {x: i for i, x in enumerate(ada_order)}
    norm_no = {x: i for i, x in enumerate([x for x in items if x[0] == "norm"])}
    glu_no = {x[1:]: i for i, x in enumerate([x for x in items if x[0] == "up"])}
    no = {kind: {x: i for i, x in enumerate([x for x in items if x[0] == kind])} for kind in {x[0] for x in items}}
    conv_no = {x: i for i, x in enumerate([x for x in items if x[0] == "proj" and x[2] in ("dq", "dk", "dv")])}
    stage_no = {x: i for i, x in enumerate([x for x in items if x[0] == "proj" and x[2] in ("z", "nq", "nk", "nv")])}
    odd_no = {x: i for i, x in enumerate([x for x in items if x[0] == "proj" and x[1] == 1])}
    pt_act_no = {x: i + 1 for i, x in enumerate([x for x in items if x[0] == "PT" and not 16 <= x[1] < 24])}
    res_no = {x: i for i, x in enumerate([x for x in items if x[0] in RESIDUAL])}
    squares = {}
    residuals = []
    for x in items:
        if x[0] in RESIDUAL:
            residuals.append(x)
        elif x[0] == "norm" and residuals:
            for i, y in enumerate(residuals[-KD:]):
                squares[y] = (norm_no[x], i)
    norm_items = [x for x in items if x[0] == "norm"]
    final = norm_items[-1]

    with ExitStack() as ctx:
        def sb(name, shape, dt=f32):
            return ctx.enter_context(nc.sbuf_tensor(name, shape, dt))

        def sem(name):
            return ctx.enter_context(nc.semaphore(name))

        h = sb("h", [P, KD, T])
        raw = [sb(f"raw{i}", [P, KD * P]) for i in range(RAW_SLOTS)]
        wh = [sb(f"wh{i}", [P, KD * P], f32r) for i in range(SPLIT_SLOTS)]
        wl = [sb(f"wl{i}", [P, KD * P], f32r) for i in range(SPLIT_SLOTS)]
        ada_raw = sb("ada_raw", [P, 2 * KD * P])
        sc = sb("sc", [P, KD, 2])
        ada_b = sb("ada_b", [P, DEPTH, N_MOD, KD])
        norm_g = sb("norm_g", [P, DEPTH * 3 + 1, KD])
        ada_tmp = sb("ada_tmp", [P, KD, 2])
        mod = sb("mod", [P, DEPTH, N_MOD, KD, 2])
        mean_w = sb("mean_w", [P, P])
        ones_w = sb("ones_w", [P, P])
        ident = sb("ident", [P, P])
        eps = sb("eps", [P, 1])
        rows = sb("rows", [P, 40])
        conv_w = sb("conv_w", [P, 12, CONV])
        dn_w = sb("dn_w", [P, 1])
        sq = [sb(f"sq{i}", [P, T]) for i in range(2)]
        sumsq = sb("sumsq", [P, T])
        std = sb("std", [P, T])
        rstd = sb("rstd", [P, T])
        nsink = sb("nsink", [P, 16])
        smx, snb, sden, ses, srec = (sb(n, [P, 56, 2]) for n in ("smx", "snb", "sden", "ses", "srec"))

        def region(name):
            guard = ExitStack()
            return guard, lambda n, shape, dt=f32: guard.enter_context(nc.sbuf_tensor(n, shape, dt))

        guard_u, ub = region("u")
        uh = ub("uh", [P, KD, T], f32r)
        ul = ub("ul", [P, KD, T], f32r)
        guard, tb = region("start")
        ada_start = [tb(f"ada_start{i}", [P, 2 * KD * P]) for i in range(ADA_FIRST)]
        guard.close()
        guard, fb = region("ffn")
        ah = fb("ah", [P, KD, T], f32r)
        al = fb("al", [P, KD, T], f32r)
        sg = [fb(f"sg{i}", [P, T]) for i in range(2)]
        af = [fb(f"af{i}", [P, T]) for i in range(2)]
        guard.close()
        guard, db = region("deltanet")
        dqkv = db("dqkv", [P, 3, DN_HEADS, T])
        o_acc = db("o_acc", [P, STEPS, 4 * P])
        masks = db("masks", [P, 4 + 2 * LEVELS, P])
        cacc = [db(f"cacc{i}", [P, T]) for i in range(2)]
        n_small = STEPS * 8
        ab, decay, beta, gc, eg, nbe, kdec, egl = (db(n, [P, STEPS, 16 if n == "ab" else 8])
                                               for n in ("ab", "g", "beta", "gc", "eg", "nbe", "kdec", "egl"))
        sp_a, sp_e, ea = db("sp_a", [P, STEPS, 8]), db("sp_e", [P, STEPS, 8]), db("ea", [P, 8])
        oss = db("oss", [P, STEPS, 4])
        guard.close()
        guard, nb = region("neighbourhood")
        nqkv = nb("nqkv", [P, 3, 4, T])
        vblk = nb("vblk", [P, 2, 4 * P])
        vctx = nb("vctx", [P, 2, 4 * P])
        bias = [nb(f"bias{i}", [P, 2, 2 * P]) for i in range(2)]
        prob_e = [nb(f"prob_e{i}", [P, 4 * P]) for i in range(4)]
        probT_e = nb("probT_e", [P, 8, P])
        otok_e = [nb(f"otok_e{i}", [P, 4 * P]) for i in range(2)]
        guard.close()
        guard, ob = region("windowed")
        sq_q = ob("sq_q", [P, KD, T_LAT])
        sw_k, sw_v = ob("sw_k", [P, 2, T]), ob("sw_v", [P, 2, T])
        sw_vt = ob("sw_vt", [P, STEPS, 2 * P])
        rope_c, rope_s = ob("rope_c", [P, T_LAT]), ob("rope_s", [P, T_LAT])
        rope_x = [ob(f"rope_x{i}", [P, T_LAT]) for i in range(2)]
        rope_p = ob("rope_p", [P, P])
        wmask = ob("wmask", [P, 2, P])
        prob_o = [ob(f"prob_o{i}", [P, 5 * P]) for i in range(4)]
        probT_o = ob("probT_o", [P, 10, P])
        otok_o = [ob(f"otok_o{i}", [P, KD * P]) for i in range(2)]
        guard.close()
        guard_u.close()
        guard, wb = region("deltanet work")
        dE, dEM, dEQ, dA, dAT, dQS = ([wb(f"{n}{i}", [P, 4, P]) for i in range(4)] for n in ("dE", "dEM", "dEQ", "dA", "dAT", "dQS"))
        guard.close()
        dX, dY, dN, dQK = dEM, dE, dA, dEQ
        dVb, dKd, dVn = dX, dN, dAT
        dS = [cacc[d][:, 0:4 * P].rearrange("p (h e) -> p h e", e=P) for d in range(2)]
        zt = [std[:, 0:4 * P], rstd[:, 0:4 * P]]
        m8 = std[:, :].rearrange("p (b k) -> p b k", b=3)
        scratch = nc.dram_tensor("spill", (16, P, T), f32, kind="Internal").ap()
        toeplitz = nc.dram_tensor("toeplitz", (16, NA_HEADS, 15, 48), f32, kind="Internal").ap()
        bias_hbm = nc.dram_tensor("bias_hbm", (3, NA_HEADS, ROWS, 16, ROWS, 32), f32, kind="Internal").ap()
        psum = ctx.enter_context(nc.psum_tensor("psum", [P, 4096], f32))

        x_loaded, c_loaded, const_loaded = sem("x_loaded"), sem("c_loaded"), sem("const_loaded")
        raw_loaded = [sem(f"raw_loaded{i}") for i in range(RAW_SLOTS)]
        start_loaded = [sem(f"start_loaded{i}") for i in range(ADA_FIRST)]
        ada_loaded = sem("ada_loaded")
        hi_split, lo_split = sem("hi_split"), sem("lo_split")
        product_done = sem("product_done")
        sc_ready, eps_set = sem("sc_ready"), sem("eps_set")
        ada_evacuated, mod_ready = sem("ada_evacuated"), sem("mod_ready")
        squared, sq_summed, std_ready, rstd_ready = sem("squared"), sem("sq_summed"), sem("std_ready"), sem("rstd_ready")
        normed, u_hi, u_lo = sem("normed"), sem("u_hi"), [sem(f"u_lo{i}") for i in range(2)]
        silu_done, glu_done, a_hi, a_lo = sem("silu_done"), sem("glu_done"), sem("a_hi"), sem("a_lo")
        h_updated = sem("h_updated")
        (conv_centre, conv_tap, convolved, staged, l2_squared, l2_std, l2_inv, l2_done, ab_read, gate_chain, gates_ready,
         cum_read, cum_scaled) = (sem(n) for n in
            "conv_centre conv_tap convolved staged l2_squared l2_std l2_inv l2_done ab_read gate_chain gates_ready cum_read cum_scaled".split())
        (dif_done, decay_ready, em_ready, eq_ready, lmat_done, a_ready, at_ready, qk_ready, x1_ready, y1_ready, n_ready, y_ready,
         x_ready, vb_ready, kd_ready, r_ready, qs_ready, vn_ready, s_ready, o_part, o_ready) = (sem("dn_" + n) for n in
            "dif_done decay_ready em_ready eq_ready lmat_done a_ready at_ready qk_ready x1_ready y1_ready n_ready y_ready x_ready vb_ready kd_ready r_ready qs_ready vn_ready s_ready o_part o_ready".split())
        (o_squared, o_summed, o_std, o_inv, o_normed, z_loaded0, z_loaded1, dny_read, dny_hi, dny_lo) = (sem("dn_" + n) for n in
            "o_squared o_summed o_std o_inv o_normed z_loaded0 z_loaded1 y_read y_hi y_lo".split())
        z_loaded = [z_loaded0, z_loaded1]
        masks_loaded, table_made, bias_made, na_loaded, m8_loaded, rope_loaded = (sem(n) for n in
            "masks_loaded table_made bias_made na_loaded m8_loaded rope_loaded".split())
        bias_loaded = [sem(f"bias_loaded{i}") for i in range(2)]
        (bias_scaled, bias_ready, max_done, neg_max, exp_done, sink_done, pt_act, pt_dve, den_done, inv_done, o_read, y_hi, y_lo,
         v_read, odd_read, rope_mul, rope_done) = (sem("at_" + n) for n in
            "bias_scaled bias_ready max_done neg_max exp_done sink_done pt_act pt_dve den_done inv_done o_read y_hi y_lo v_read odd_read rope_mul rope_done".split())
        sink_sum = sem("sink_sum")
        sink_neg, v_gathered, abs_done = sem("sink_neg"), sem("v_gathered"), sem("dn_abs_done")
        spilled_by = [sem(f"spilled_by{i}") for i in range(2)]
        out_ready, out_stored = sem("out_ready"), [sem(f"out_stored{i}") for i in range(2)]

        def work(x):
            return 2 * (x[1] % 2) + x[2]

        def group(x):
            return 2 * x[1] + x[2]

        def released(x):
            kind = x[0]
            n = no[kind][x] + 1
            if kind == "proj":
                if x in conv_no:
                    return [(conv_tap, 4 * conv_no[x] + 4)]
                if x in stage_no:
                    return [(staged, stage_no[x] + 1)]
                return [(ab_read, 1)] if x[2] == "ab" else [(odd_read, odd_no[x] + 1)]
            if kind in RESIDUAL:
                return [(h_updated, res_no[x] + 1)]
            if kind == "dnK":
                return [(r_ready, group(x) - 1), (qs_ready, group(x) - 1)]
            if kind == "PT":
                return [(pt_dve, n)] + ([(pt_act, pt_act_no[x])] if x in pt_act_no else [])
            if kind == "cum":
                return [(cum_read, 2)]
            if kind == "dnT":
                return [(at_ready, n), (qk_ready, n)]
            return [({"ada": ada_evacuated, "norm": std_ready, "gate": silu_done, "up": glu_done, "l2": l2_std,
                      "cum": cum_read, "dnA": lmat_done, "dnN": n_ready, "dnY": y_ready, "dnX": x_ready, "dnV": kd_ready,
                      "dnU": vn_ready, "dnO": o_ready, "dny": dny_read, "vt": v_read, "rope": rope_done, "S": exp_done,
                      "O": o_read, "Y": y_lo}[kind], n)]

        place, turn = {}, 0
        for x in items:
            kind, in_scan = x[0], x[0] == "ada" and x[1] == 1 and ("dnA", 0, 0) in number
            if kind in ("dnA", "dnT"):
                place[x] = (2 * x[2], 2)
            elif kind in ("dnN", "dnX", "dnY"):
                place[x] = (2 * x[2] + (kind == "dnY"), 1)
            elif kind in ("dnV", "dnK", "dnU", "dnO"):
                place[x] = (4 + 2 * x[2], 1 if kind == "dnU" else 2)
            elif in_scan:
                place[x] = (5 + 2 * (x[3] % 2), 1)
            elif kind == "S":
                place[x] = (2 * x[2], 2) if x[1] >= 24 else (2 * x[2] + x[1] % 2, 1)
            elif kind == "PT":
                place[x] = (4, 3 if x[1] >= 24 else 2 if x[1] < 16 else 1)
            elif kind == "O":
                place[x] = (7, 1)
            elif kind == "Y":
                place[x] = (4, 2 if x[1] >= 6 else 1)
            elif kind == "vt":
                place[x] = (4, 2)
            else:
                place[x] = (2 * (turn % 4), 2)
                turn += 1
        tenants, before = {}, {}
        for x in items:
            banks = range(place[x][0], sum(place[x]))
            before[x] = list(dict.fromkeys(tenants[b] for b in banks if b in tenants))
            tenants.update({b: x for b in banks})

        def banks_of(x):
            return psum[:, 512 * place[x][0]:512 * sum(place[x])]

        def segs_of(x):
            if x[0] in ("gate", "up", "down"):
                return segments(x[1], x[2])
            if x[0] == "norm":
                return [LAT] if x[1] >= 5 else [LAT, CTX]
            return [LAT] if x[:2] == ("out", 1) or x[:3] == ("proj", 1, "q") else [LAT, CTX]

        def x_before(*match):
            at = next(i for i, x in enumerate(items) if x[:len(match)] == match)
            return [y for y in items[:at] if y[0] in RESIDUAL][-1]

        CONSTS = 16 * 8

        def gate_term(x):
            return 5 if x[0] == "out" else 3 * (2 * x[2]) + 2

        def u_source(x):
            return norm_no[[y for y in norm_items if number[y] < number[x]][-1]]

        def attention(u, a_):
            half = slice(HD * a_, HD * a_ + HD)
            if u < 16:
                jb, i = divmod(u, 4)
                c0 = [0, 8, 24, 32][jb]
                grid = lambda w: nqkv[half, w, i, 0:T_LAT].rearrange("p (r c) -> p r c", c=GRID_W)
                q = nqkv[half, 0, i, P * jb:P * jb + P]
                keys = [(0, 2 * P, grid(1)[:, :, c0:c0 + 32], bias[u % 2][:, a_, :]),
                        (2 * P, 2 * P, nqkv[half, 1, i, T_LAT:T], None)]
                f = slice(P * i + HD * a_, P * i + HD * a_ + HD)
                return q, keys, [vblk[:, 0, f], vblk[:, 1, f], vctx[:, 0, f], vctx[:, 1, f]]
            if u < 24:
                qb, i = divmod(u - 16, 4)
                f = slice(P * i + HD * a_, P * i + HD * a_ + HD)
                return (nqkv[half, 0, i, T_LAT + P * qb:T_LAT + P * qb + P], [(0, 2 * P, nqkv[half, 1, i, T_LAT:T], None)],
                        [vctx[:, 0, f], vctx[:, 1, f]])
            n, t = divmod(u - 24, KD)
            tiles = [m for m in (n - 1, n, n + 1) if 0 <= m < 4] + [4, 5]
            side = {n - 1: wmask[:, 0, :], n + 1: wmask[:, 1, :]}
            keys = [(P * j, P, sw_k[half, t // 4, P * m:P * m + P], side.get(m) if m < 4 else None) for j, m in enumerate(tiles)]
            f = slice(P * (t // 4) + HD * a_, P * (t // 4) + HD * a_ + HD)
            return sq_q[half, t, P * n:P * n + P], keys, [sw_vt[:, m, f] for m in tiles]

        def width(u):
            return P * len(attention(u, 0)[2])

        def prob(u, a_):
            return (prob_e if u < 24 else prob_o)[2 * (u % 2) + a_]

        def probT(u):
            return (probT_e if u < 24 else probT_o)[:, 0:2 * width(u) // P, :]

        def otok(b):
            return (otok_e if b < 6 else otok_o)[b % 2]

        def tile_of(u):
            return u % 4 if u < 24 else (u - 24) % KD

        def y_target(t, b):
            if b < 4:
                return t[:, 0:4, 0:T_LAT].rearrange("p k (r c) -> p k r c", c=GRID_W)[:, :, :, 16 * b:16 * b + 16]
            if b < 6:
                return t[:, 0:4, T_LAT + P * (b - 4):T_LAT + P * (b - 4) + P]
            return t[:, :, P * (b - 6):P * (b - 6) + P]

        def y_source(pair, b):
            if b < 4:
                return pair[:, 0:4 * P].rearrange("p (k r c) -> p k r c", k=4, c=16)
            return pair[:, 0:(4 if b < 6 else KD) * P].rearrange("p (k q) -> p k q", q=P)

        def per_head(t, tile, d):
            return t[:, tile, 4 * d:4 * d + 4].unsqueeze(2).to_broadcast([P, 4, P])

        def over_heads(m):
            return masks[:, m, :].unsqueeze(1).to_broadcast([P, 4, P])

        v_cols = lambda f: sq[f // 2][:, 2 * P * (f % 2):2 * P * (f % 2) + 2 * P]
        l2_items = list(no.get("l2", {}))
        rope_items = [x for x in odd_no if x[2] in ("k", "q")]
        rope_no = rope_items.index
        o_part_no = {x: j for j, x in enumerate(
            [x for x in items if x[0] == "dnO" and not (SCAN[1 - x[2]].index(SCAN[x[2]][x[1]]) > x[1])])}
        y_tmp = lambda t: cacc[t % 2][:, 0:4 * P].rearrange("p (k q) -> p k q", q=P)

        def normed_tile(k):
            return sq[0] if k % 2 == 0 else (sq[1], std)[k // 2 % 2]

        def low_part(engine, wait_ge, x, k):
            m, layer, s = norm_no[x], x[1] // 3, x[1] % 3
            wait_ge(u_hi, KD * m + k + 1)
            for v, (lo, hi) in enumerate(segs_of(x)):
                ins = engine.scalar_tensor_tensor(out=ul[:, k, lo:hi], in0=normed_tile(k)[:, lo:hi],
                                                  scalar=mod[:, layer, 3 * s, k, v:v + 1],
                                                  in1=uh[:, k, lo:hi].bitcast(f32), op0=ALU.add, op1=ALU.subtract)
            ins.then_inc(u_lo[k % 2], 1)

        def l2_after(x):
            if not l2_items:
                return None
            at = number[x]
            ahead = [j for j, y in enumerate(l2_items) if number[y] == at + 4]
            return ahead[0] if ahead else None

        U, STRICT, LEVEL = [0, 1], [2, 3], [4, 4 + LEVELS]

        def pair4(pair, half):
            return pair[:, 512 * half:512 * half + 512].rearrange("p (h s) -> p h s", s=P)

        block = ctx.enter_context(nc.Block())

        @block.sync
        def _(sp):
            sp.dma_start(h[:, :, :], a["xT"]).then_inc(x_loaded, 16)
            sp.dma_start(sc[:, :, :], a["cT"]).then_inc(c_loaded, 16)
            sp.dma_start(ada_b[:, :, :, :], a["ada_bT"]).then_inc(const_loaded, 16)
            sp.dma_start(norm_g[:, :, :], a["norm_gT"]).then_inc(const_loaded, 16)
            sp.dma_start(mean_w[:, :], a["mean_w"]).then_inc(const_loaded, 16)
            sp.dma_start(ones_w[:, :], a["ones_w"]).then_inc(const_loaded, 16)
            sp.dma_start(ident[:, :], a["ident"]).then_inc(const_loaded, 16)
            sp.dma_start(rows[:, :], a["rows"].to_broadcast([P, 40])).then_inc(const_loaded, 16)
            sp.dma_start(conv_w[:, :, :], a["conv_w"]).then_inc(const_loaded, 16)
            sp.dma_start(dn_w[:, :], a["dn_w"]).then_inc(const_loaded, 16)
            nada = 0
            windows = [(o, r, hd) for o in range(3) for r in range(ROWS) for hd in range(NA_HEADS)]

            def table(c):
                sp.dma_start(toeplitz[c], a["rpb"][:, :, 15 - c:63 - c]).then_inc(table_made, 16)

            def window(o, r, hd):
                sp.dma_start(bias_hbm[o, hd, r], toeplitz[:, hd, ROWS - 1 - r:2 * ROWS - 1 - r, 16 - 8 * o:48 - 8 * o]) \
                    .then_inc(bias_made, 16)

            def load_bias(u):
                jb, i = divmod(u, 4)
                sp.dma_start(bias[u % 2][:, :, :], bias_hbm[[0, 1, 1, 2][jb], 2 * i:2 * i + 2]
                             .rearrange("h r c a k -> (r c) h (a k)")).then_inc(bias_loaded[u % 2], 16)

            for x in items:
                if x[0] == "ada":
                    n = ada_no[x]
                    if n < ADA_FIRST:
                        sp.dma_start(ada_start[n][:, :], a["ada_w"][x[1], x[2], x[3]]).then_inc(start_loaded[n], 16)
                    else:
                        if n > ADA_FIRST:
                            sp.wait_ge(product_done, number[ada_order[n - 1]] + 1)
                        sp.dma_start(ada_raw[:, :], a["ada_w"][x[1], x[2], x[3]]).then_inc(ada_loaded, 16)
                elif x in slot_of:
                    n = slot_of[x]
                    _, k, w = slots[n]
                    if n >= RAW_SLOTS:
                        sp.wait_ge(lo_split, n - RAW_SLOTS + 1)
                    src = a["w"][slot_at[n]:slot_at[n + 1]].rearrange("(p c) -> p c", p=P)
                    sp.dma_start(raw[n % RAW_SLOTS][:, 0:k * w], src).then_inc(raw_loaded[n % RAW_SLOTS], 16)
                if x[0] in ("gate", "up") and x[1:3] == (0, 0) and "dnA" in no:
                    if x[5] < 8:
                        table(2 * x[5] + (x[0] == "up"))
                    elif windows:
                        if x[5] == 8 and x[0] == "gate":
                            sp.wait_ge(table_made, 16 * 16)
                        for wnd in windows[:7]:
                            window(*wnd)
                        windows = windows[7:]
                if x == ("proj", 0, "dq", 0):
                    sp.wait_ge(h_updated, KD * len(PARTS))
                    sp.dma_start(masks[:, :, :], a["masks"]).then_inc(masks_loaded, 16)
                if x[0] == "dny":
                    t = x[1]
                    if t == 0:
                        for half in range(2):
                            sp.wait_ge(spilled_by[half], 16 * 8)
                        sp.wait_ge(l2_done, 8)
                    if t >= 2:
                        sp.wait_ge(dny_read, t - 1)
                    sp.dma_start(zt[t % 2].rearrange("p (k q) -> p k q", q=P),
                                 scratch[0:4, :, P * t:P * t + P].rearrange("k p q -> p k q")).then_inc(z_loaded[t % 2], 16)
                if x[0] == "vt" and x == ("vt", 0, 4):
                    sp.wait_ge(dny_lo, STEPS)
                    for w in range(3):
                        sp.dma_start(nqkv[:, w, :, :], scratch[4 + 4 * w:8 + 4 * w].rearrange("k p t -> p k t")) \
                            .then_inc(na_loaded, 16)
                    sp.dma_start(m8[:, :, :], a["m8"]).then_inc(m8_loaded, 16)
                    sp.wait_ge(bias_made, 16 * 3 * ROWS * NA_HEADS)
                    load_bias(0)
                    load_bias(1)
                if x[0] == "O" and x[1] < 14:
                    sp.wait_ge(product_done, number[("S", x[1], 1)] + 1)
                    load_bias(x[1] + 2)
                if x == ("proj", 1, "k", 0):
                    sp.wait_ge(h_updated, res_no[x_before("proj", 1)] + 1)
                    for dst, src in ((rope_c, "rope_c"), (rope_s, "rope_s"), (rope_p, "rope_p"), (wmask, "wmask")):
                        sp.dma_start(dst[(slice(None),) * len(dst.shape)], a[src]).then_inc(rope_loaded, 16)
            for i in range(KD):
                sp.wait_ge(out_ready, i + 1)
                sp.dma_start(out[i], sq[i % 2][:, 0:T_LAT]).then_inc(out_stored[i % 2], 16)
            for i in range(2):
                sp.wait_ge(out_stored[i], 16 * KD // 2)

        @block.gpsimd
        def _(pool):
            nc.gpsimd.memset(eps[:, :], EPS).then_inc(eps_set, 1)
            done = [0]

            def split_up_to(n_slots):
                while done[0] < min(n_slots, len(slots)):
                    n = done[0]
                    _, k, w = slots[n]
                    pool.wait_ge(hi_split, n + 1)
                    nc.gpsimd.tensor_tensor(wl[n % SPLIT_SLOTS][:, 0:k * w], raw[n % RAW_SLOTS][:, 0:k * w],
                                            wh[n % SPLIT_SLOTS][:, 0:k * w].bitcast(f32), ALU.subtract).then_inc(lo_split, 1)
                    done[0] += 1

            for x in items:
                split_up_to(sum(number[y] <= number[x] + 2 for y, _, _ in slots))
                if x[0] == "dnA":
                    d, n, b = x[2], group(x), work(x)
                    pool.wait_ge(decay_ready, n + 1)
                    if n == 0:
                        pool.wait_ge(masks_loaded, 16)
                    nc.gpsimd.tensor_tensor(dEM[b][:, :, :], dE[b][:, :, :], over_heads(STRICT[d]), ALU.mult).then_inc(em_ready, 1)
                    nc.gpsimd.tensor_tensor(dEQ[b][:, :, :], dE[b][:, :, :], over_heads(U[d]), ALU.mult).then_inc(eq_ready, 1)
                elif x[0] == "dnT":
                    d, n, b = x[2], group(x), work(x)
                    pool.wait_ge(a_ready, n + 1)
                    nc.gpsimd.tensor_tensor(dX[b][:, :, :], dA[b][:, :, :], over_heads(LEVEL[d]), ALU.mult).then_inc(x1_ready, 1)
                    pool.wait_ge(at_ready, n + 1)
                    pool.wait_ge(eq_ready, n + 1)
                    nc.gpsimd.tensor_tensor(dY[b][:, :, :], dAT[b][:, :, :], over_heads(LEVEL[1 - d]), ALU.mult).then_inc(y1_ready, 1)
                elif x == ("dny", 0):
                    for t in range(STEPS):
                        if t < 2:
                            pool.wait_ge(o_ready, 2 * STEPS)
                            pool.wait_ge(spilled_by[t], 16 * 8)
                        if t >= 2:
                            pool.wait_ge(o_summed, t - 1)
                        nc.gpsimd.tensor_tensor(cacc[t % 2][:, 0:4 * P], o_acc[:, t, :], o_acc[:, t, :], ALU.mult).then_inc(o_squared, 1)
                elif x[0] == "vt" and x[1] == 0 and x[2] < 4:
                    jb = x[2]
                    pool.wait_ge(na_loaded, 48)
                    pool.wait_ge(product_done, number[("vt", 0, jb - 1 if jb else 4)] + 1)
                    c0 = [0, 8, 24, 32][jb]
                    for f in range(4):
                        ins = nc.gpsimd.tensor_copy(v_cols(f).rearrange("p (r c) -> p r c", c=32),
                                                    nqkv[:, 2, f, 0:T_LAT].rearrange("p (r c) -> p r c", c=GRID_W)[:, :, c0:c0 + 32])
                    ins.then_inc(v_gathered, 1)
                elif x[0] == "S" and x[1] < 16 and x[2] == 0:
                    u = x[1]
                    pool.wait_ge(bias_loaded[u % 2], 16 * (u // 2 + 1))
                    if u == 0:
                        pool.wait_ge(m8_loaded, 16)
                    b = bias[u % 2][:, :, :]
                    nc.gpsimd.tensor_scalar(b, b, float(HD) ** 0.5, None, ALU.mult).then_inc(bias_scaled, 1)
                    pool.wait_ge(bias_scaled, u + 1)
                    nc.gpsimd.tensor_tensor(b, b, m8[:, [0, 1, 1, 2][u // 4], :].unsqueeze(1).to_broadcast([P, 2, 2 * P]),
                                            ALU.add).then_inc(bias_ready, 1)

        @block.scalar
        def _(act):
            done = [0]

            def split_up_to(n_slots):
                while done[0] < min(n_slots, len(slots)):
                    n = done[0]
                    _, k, w = slots[n]
                    act.wait_ge(raw_loaded[n % RAW_SLOTS], 16 * (n // RAW_SLOTS + 1))
                    if n >= SPLIT_SLOTS:
                        act.wait_ge(product_done, number[slots[n - SPLIT_SLOTS][0]] + 1)
                    nc.scalar.activation(wh[n % SPLIT_SLOTS][:, 0:k * w], raw[n % RAW_SLOTS][:, 0:k * w],
                                         ACT.Copy).then_inc(hi_split, 1)
                    done[0] += 1

            def square(m, i):
                k = KD * m + i
                if k >= 2:
                    act.wait_ge(sq_summed, k - 1)
                nc.scalar.activation(sq[i % 2][:, :], h[:, i, :], ACT.Square).then_inc(squared, 1)

            act.wait_ge(c_loaded, 16)
            nc.scalar.activation(ada_tmp[:, :, :], sc[:, :, :], ACT.Sigmoid).then_inc(sc_ready, 1)
            act.wait_ge(x_loaded, 16)
            act.wait_ge(eps_set, 1)
            for i in range(KD):
                square(0, i)
            for x in items:
                i = number[x]
                split_up_to(sum(number[y] <= i + 2 for y, _, _ in slots))
                if x[0] == "norm":
                    m = norm_no[x]
                    last = segs_of(x)[-1][1]
                    act.wait_ge(product_done, i + 1)
                    if m:
                        act.wait_ge(rstd_ready, m)
                    nc.scalar.activation(std[:, 0:last], banks_of(x)[:, 0:last], ACT.Sqrt,
                                         bias=eps[:, :]).then_inc(std_ready, 1)
                    if x != final:
                        layer, s = x[1] // 3, x[1] % 3
                        for k in range(KD):
                            act.wait_ge(normed, KD * m + k + 1)
                            for v, (lo, hi) in enumerate(segs_of(x)):
                                ins = nc.scalar.activation(uh[:, k, lo:hi], normed_tile(k)[:, lo:hi], ACT.Identity,
                                                           bias=mod[:, layer, 3 * s, k, v:v + 1])
                            ins.then_inc(u_hi, 1)
                elif x[0] == "gate":
                    g = glu_no[x[1:]]
                    last = segs_of(x)[-1][1]
                    act.wait_ge(product_done, i + 1)
                    if g >= 2:
                        act.wait_ge(glu_done, g - 1)
                    nc.scalar.activation(sg[g % 2][:, 0:last], banks_of(x)[:, 0:last], ACT.Silu).then_inc(silu_done, 1)
                elif x[0] == "up":
                    g, c = glu_no[x[1:]], x[4]
                    last = segs_of(x)[-1][1]
                    act.wait_ge(glu_done, g + 1)
                    nc.scalar.activation(ah[:, c, 0:last], af[g % 2][:, 0:last], ACT.Copy).then_inc(a_hi, 1)
                elif x in conv_no:
                    c = conv_no[x]
                    act.wait_ge(product_done, i + 1)
                    if c == 0:
                        act.wait_ge(const_loaded, CONSTS)
                    if c >= 2:
                        act.wait_ge(convolved, c - 1)
                    nc.scalar.activation(cacc[c % 2][:, :], banks_of(x)[:, 0:T], ACT.Copy,
                                         scale=conv_w[:, c, 2:3]).then_inc(conv_centre, 1)
                    act.wait_ge(conv_tap, 4 * c + 4)
                    nc.scalar.activation(dqkv[:, c // 4, c % 4, :], cacc[c % 2][:, :], ACT.Silu).then_inc(convolved, 1)
                elif x in stage_no:
                    c = stage_no[x]
                    act.wait_ge(product_done, i + 1)
                    if c == 0:
                        act.wait_ge(convolved, 12)
                    if c >= 2:
                        act.wait_ge(spilled_by[c % 2], 16 * (c // 2))
                    if x[2] == "nq":
                        for jb in range(4):
                            nc.scalar.activation(cacc[c % 2][:, P * jb:P * jb + P].rearrange("p (r c) -> p r c", c=16),
                                                 banks_of(x)[:, 0:T_LAT].rearrange("p (r c) -> p r c", c=GRID_W)
                                                 [:, :, 16 * jb:16 * jb + 16], ACT.Copy)
                        nc.scalar.activation(cacc[c % 2][:, T_LAT:T], banks_of(x)[:, T_LAT:T], ACT.Copy).then_inc(staged, 1)
                    else:
                        nc.scalar.activation(cacc[c % 2][:, :], banks_of(x)[:, 0:T], ACT.Silu if x[2] == "z" else ACT.Copy) \
                            .then_inc(staged, 1)
                    act.wait_ge(staged, c + 1)
                    act.dma_start(scratch[c], cacc[c % 2][:, :]).then_inc(spilled_by[c % 2], 16)
                elif x[0] == "l2":
                    j = no["l2"][x]
                    act.wait_ge(product_done, i + 1)
                    if j:
                        act.wait_ge(l2_inv, j)
                    nc.scalar.activation(std[:, :], banks_of(x)[:, 0:T], ACT.Sqrt, bias=eps[:, :]).then_inc(l2_std, 1)
                elif x[0] == "cum":
                    act.wait_ge(ab_read, 1)
                    nc.scalar.activation(sp_a[:, :, :], ab[:, :, 0:8], ACT.Abs).then_inc(gate_chain, 1)
                    act.wait_ge(gate_chain, 1)
                    nc.scalar.activation(sp_e[:, :, :], sp_a[:, :, :], ACT.Exp, scale=-1.0).then_inc(gate_chain, 1)
                    act.wait_ge(gate_chain, 2)
                    nc.scalar.activation(sp_a[:, :, :], sp_e[:, :, :], ACT.Ln, bias=1.0).then_inc(gate_chain, 1)
                    nc.scalar.activation(ea[:, :], rows[:, 0:8], ACT.Exp).then_inc(gate_chain, 1)
                    nc.scalar.activation(beta[:, :, :], ab[:, :, 8:16], ACT.Sigmoid).then_inc(gate_chain, 1)
                    act.wait_ge(product_done, i + 1)
                    nc.scalar.activation(eg[:, :, :], banks_of(x)[:, 0:48].rearrange("p (t c) -> p t c", c=8), ACT.Exp)
                    nc.scalar.activation(egl[:, :, :], banks_of(x)[:, 48:96].rearrange("p (t c) -> p t c", c=8),
                                         ACT.Exp).then_inc(cum_read, 1)
                    act.wait_ge(cum_scaled, 2)
                    nc.scalar.activation(kdec[:, :, :], kdec[:, :, :], ACT.Exp).then_inc(cum_scaled, 1)
                elif x[0] == "dnA":
                    d, n, b = x[2], group(x), work(x)
                    act.wait_ge(dif_done, n + 1)
                    nc.scalar.activation(dE[b][:, :, :], dE[b][:, :, :], ACT.Abs).then_inc(abs_done, 1)
                    act.wait_ge(abs_done, n + 1)
                    nc.scalar.activation(dE[b][:, :, :], dE[b][:, :, :], ACT.Exp, scale=-1.0).then_inc(decay_ready, 1)
                elif x[0] == "dnT":
                    act.wait_ge(product_done, i + 1)
                    nc.scalar.activation(dAT[work(x)][:, :, :], pair4(banks_of(x), 0), ACT.Copy).then_inc(at_ready, 1)
                elif x[0] == "dnY":
                    act.wait_ge(product_done, i + 1)
                    nc.scalar.activation(dY[work(x)][:, :, :], pair4(banks_of(x), 0), ACT.Copy).then_inc(y_ready, 1)
                elif x[0] == "dnK":
                    d, tile, b = x[2], SCAN[x[2]][x[1]], work(x)
                    act.wait_ge(product_done, i + 1)
                    for hd in range(4):
                        ins = nc.scalar.activation(dQS[b][:, hd, :], pair4(banks_of(x), 1)[:, hd, :], ACT.Copy,
                                                   scale=eg[:, tile, 4 * d + hd:4 * d + hd + 1])
                    ins.then_inc(qs_ready, 1)
                elif x[0] == "dnU":
                    act.wait_ge(product_done, i + 1)
                    nc.scalar.activation(dVn[work(x)][:, :, :], pair4(banks_of(x), 0), ACT.Copy).then_inc(vn_ready, 1)
                elif x[0] == "dny":
                    t = x[1]
                    if t == 0:
                        act.wait_ge(o_summed, STEPS)
                        nc.scalar.activation(oss[:, :, :], oss[:, :, :], ACT.Sqrt, bias=eps[:, :], scale=1.0 / P).then_inc(o_std, 1)
                    act.wait_ge(dny_read, t + 1)
                    nc.scalar.activation(uh[:, 4:8, P * t:P * t + P], y_tmp(t), ACT.Copy).then_inc(dny_hi, 1)
                elif x[0] == "vt":
                    act.wait_ge(product_done, i + 1)
                    if x[1] == 0:
                        dst = vctx if x[2] == 4 else vblk
                        nc.scalar.activation(dst[:, :, :].rearrange("p c f -> p (c f)"), banks_of(x)[:, :], ACT.Copy).then_inc(v_read, 1)
                    else:
                        nc.scalar.activation(sw_vt[:, 3 * x[2]:3 * x[2] + 3, :].rearrange("p c f -> p (c f)"),
                                             banks_of(x)[:, 0:6 * P], ACT.Copy).then_inc(v_read, 1)
                elif x in odd_no:
                    c = odd_no[x]
                    act.wait_ge(product_done, i + 1)
                    if x[2] == "v":
                        nc.scalar.activation(sw_v[:, x[3], :], banks_of(x)[:, 0:T], ACT.Copy).then_inc(odd_read, 1)
                    else:
                        r = rope_no(x)
                        if r >= 2:
                            act.wait_ge(rope_done, r - 1)
                        if x[2] == "k":
                            nc.scalar.activation(sw_k[:, x[3], T_LAT:T], banks_of(x)[:, T_LAT:T], ACT.Copy)
                        nc.scalar.activation(rope_x[r % 2][:, :], banks_of(x)[:, 0:T_LAT], ACT.Copy).then_inc(odd_read, 1)
                elif x[0] == "S":
                    u, a_ = x[1], x[2]
                    w = width(u)
                    act.wait_ge(neg_max, 2 * u + a_ + 1)
                    if u >= 2:
                        act.wait_ge(product_done, number[("PT", u - 2)] + 1)
                    nc.scalar.activation(prob(u, a_)[:, 0:w], banks_of(x)[:, 0:w], ACT.Exp, bias=snb[:, u, a_:a_ + 1],
                                         scale=float(HD) ** -0.5, accum_out=sden[:, u, a_:a_ + 1]).then_inc(exp_done, 1)
                elif x[0] == "PT":
                    u = x[1]
                    if x in pt_act_no:
                        act.wait_ge(product_done, i + 1)
                        if u >= 1:
                            act.wait_ge(product_done, number[("O", u - 1)] + 1)
                        n = 2 * width(u) // P
                        nc.scalar.activation(probT(u)[:, 4:n, :], banks_of(x)[:, 4 * P:n * P].rearrange("p (c q) -> p c q", q=P),
                                             ACT.Copy).then_inc(pt_act, 1)
                    if u >= 24:
                        act.wait_ge(sink_sum, u - 23)
                        nc.scalar.activation(ses[:, u, :], ses[:, u, :], ACT.Exp).then_inc(sink_done, 1)
                elif x[0] == "Y":
                    b = x[1]
                    act.wait_ge(product_done, i + 1)
                    for k in range(4 if b < 6 else KD):
                        ins = nc.scalar.activation(y_target(uh, b)[:, k], y_source(banks_of(x), b)[:, k], ACT.Copy)
                    ins.then_inc(y_hi, 1)
                if x[0] in ("proj", "l2") and l2_after(x) is not None:
                    j = l2_after(x)
                    act.wait_ge(convolved, 12)
                    if j >= 2:
                        act.wait_ge(product_done, number[l2_items[j - 2]] + 1)
                    nc.scalar.activation(sq[j % 2][:, :], dqkv[:, j // 4, j % 4, :], ACT.Square).then_inc(l2_squared, 1)
                if x in squares:
                    act.wait_ge(h_updated, res_no[x] + 1)
                    square(*squares[x])

        @block.vector
        def _(dve):
            dve.wait_ge(sc_ready, 1)
            nc.vector.tensor_tensor(sc[:, :, :], sc[:, :, :], ada_tmp[:, :, :], ALU.mult).then_inc(sc_ready, 1)
            dve.wait_ge(const_loaded, CONSTS)

            def add_square(m, i):
                k = KD * m + i
                dve.wait_ge(squared, k + 1)
                if i == 0:
                    nc.vector.tensor_copy(sumsq[:, :], sq[0][:, :]).then_inc(sq_summed, 1)
                else:
                    dve.wait_ge(sq_summed, k)
                    nc.vector.tensor_tensor(sumsq[:, :], sumsq[:, :], sq[i % 2][:, :], ALU.add).then_inc(sq_summed, 1)

            def a_matrix(x):
                d, n, tile, b = x[2], group(x), SCAN[x[2]][x[1]], work(x)
                dve.wait_ge(em_ready, n + 1)
                for hd in range(4):
                    ins = nc.vector.scalar_tensor_tensor(out=dA[b][:, hd, :], in0=pair4(banks_of(x), 1)[:, hd, :],
                                                         scalar=beta[:, tile, 4 * d + hd:4 * d + hd + 1],
                                                         in1=dEM[b][:, hd, :], op0=ALU.mult, op1=ALU.mult)
                ins.then_inc(lmat_done, 1)
                dve.wait_ge(lmat_done, n + 1)
                nc.vector.tensor_tensor(dA[b][:, :, :], dA[b][:, :, :], ident[:, :].unsqueeze(1).to_broadcast([P, 4, P]),
                                        ALU.add).then_inc(a_ready, 1)

            for i in range(KD):
                add_square(0, i)
            for x in items:
                i = number[x]
                if x[0] == "ada":
                    n, t, two = ada_no[x], x[2], slice(2 * x[3], 2 * x[3] + 2)
                    spread_out = lambda v: v.unsqueeze(2).to_broadcast([P, 2, 2])
                    tmp = ada_tmp[:, 0:2, :]
                    dve.wait_ge(product_done, i + 1)
                    if n:
                        dve.wait_ge(mod_ready, n)
                    nc.vector.tensor_tensor(tmp, banks_of(x)[:, 0:4].rearrange("p (k v) -> p k v", v=2),
                                            spread_out(ada_b[:, x[1], t, two]), ALU.add).then_inc(ada_evacuated, 1)
                    dve.wait_ge(ada_evacuated, n + 1)
                    dst = mod[:, x[1], t, two, :]
                    if t % 3 == 0:
                        nc.vector.tensor_copy(dst, tmp).then_inc(mod_ready, 1)
                    elif t % 3 == 1:
                        nc.vector.scalar_tensor_tensor(out=dst, in0=tmp, scalar=1.0, in1=spread_out(norm_g[:, 3 * x[1] + t // 3, two]),
                                                       op0=ALU.add, op1=ALU.mult).then_inc(mod_ready, 1)
                    else:
                        nc.vector.tensor_scalar(dst, tmp, 1.0 if t == 5 else 0.5, None, ALU.mult).then_inc(mod_ready, 1)
                elif x[0] == "norm":
                    m = norm_no[x]
                    last = segs_of(x)[-1][1]
                    layer, s = x[1] // 3, x[1] % 3
                    dve.wait_ge(std_ready, m + 1)
                    nc.vector.reciprocal(rstd[:, 0:last], std[:, 0:last]).then_inc(rstd_ready, 1)
                    dve.wait_ge(rstd_ready, m + 1)
                    if x != final:
                        dve.wait_ge(mod_ready, max(ada_no[("ada", layer, 3 * s + t, ADA_SPLIT - 1)] for t in range(2)) + 1)
                    for k in range(KD):
                        if x == final:
                            if k >= 2:
                                dve.wait_ge(out_stored[k % 2], 16 * (k // 2))
                            nc.vector.scalar_tensor_tensor(out=sq[k % 2][:, 0:last], in0=h[:, k, 0:last],
                                                           scalar=norm_g[:, 3 * DEPTH, k:k + 1], in1=rstd[:, 0:last],
                                                           op0=ALU.mult, op1=ALU.mult).then_inc(out_ready, 1)
                            continue
                        if k >= 2 and k % 2 == 0:
                            dve.wait_ge(u_lo[0], KD // 2 * m + k // 2)
                        elif k >= 4:
                            dve.wait_ge(u_lo[1], KD // 2 * m + k // 2 - 1)
                        for v, (lo, hi) in enumerate(segs_of(x)):
                            ins = nc.vector.scalar_tensor_tensor(out=normed_tile(k)[:, lo:hi], in0=h[:, k, lo:hi],
                                                                 scalar=mod[:, layer, 3 * s + 1, k, v:v + 1],
                                                                 in1=rstd[:, lo:hi], op0=ALU.mult, op1=ALU.mult)
                        ins.then_inc(normed, 1)
                        if k:
                            low_part(nc.vector, dve.wait_ge, x, k - 1)
                    if x != final:
                        low_part(nc.vector, dve.wait_ge, x, KD - 1)
                elif x[0] == "up":
                    g, c = glu_no[x[1:]], x[4]
                    last = segs_of(x)[-1][1]
                    dve.wait_ge(product_done, i + 1)
                    dve.wait_ge(silu_done, g + 1)
                    if g >= 2:
                        dve.wait_ge(a_lo, g - 1)
                    nc.vector.tensor_tensor(af[g % 2][:, 0:last], sg[g % 2][:, 0:last], banks_of(x)[:, 0:last],
                                            ALU.mult).then_inc(glu_done, 1)
                    dve.wait_ge(a_hi, g + 1)
                    nc.vector.tensor_tensor(al[:, c, 0:last], af[g % 2][:, 0:last], ah[:, c, 0:last].bitcast(f32),
                                            ALU.subtract).then_inc(a_lo, 1)
                elif x in conv_no:
                    c = conv_no[x]
                    dve.wait_ge(conv_centre, c + 1)
                    for n, j in enumerate((0, 1, 3, 4)):
                        sh = j - 2
                        if n:
                            dve.wait_ge(conv_tap, 4 * c + n)
                        for lo, hi in (LAT, CTX):
                            dst = (lo - min(sh, 0), hi - max(sh, 0))
                            acc = cacc[c % 2][:, dst[0]:dst[1]]
                            ins = nc.vector.scalar_tensor_tensor(out=acc, in0=banks_of(x)[:, dst[0] + sh:dst[1] + sh],
                                                                 scalar=conv_w[:, c, j:j + 1], in1=acc, op0=ALU.mult, op1=ALU.add)
                        ins.then_inc(conv_tap, 1)
                elif x[0] == "proj" and x[2] == "ab":
                    dve.wait_ge(product_done, i + 1)
                    nc.vector.tensor_tensor(ab[:, :, :], banks_of(x)[:, 0:96].rearrange("p (t c) -> p t c", c=16),
                                            rows[:, 8:24].unsqueeze(1).to_broadcast([P, STEPS, 16]), ALU.add).then_inc(ab_read, 1)
                elif x[0] == "l2":
                    j = no["l2"][x]
                    dve.wait_ge(l2_std, j + 1)
                    if j:
                        dve.wait_ge(l2_done, j)
                    nc.vector.reciprocal(rstd[:, :], std[:, :]).then_inc(l2_inv, 1)
                    dve.wait_ge(l2_inv, j + 1)
                    qk = dqkv[:, j // 4, j % 4, :]
                    nc.vector.scalar_tensor_tensor(out=qk, in0=rstd[:, :], scalar=float(P) ** -0.5 if j < 4 else 1.0, in1=qk,
                                                   op0=ALU.mult, op1=ALU.mult).then_inc(l2_done, 1)
                elif x[0] == "cum":
                    dve.wait_ge(gate_chain, 5)
                    nc.vector.scalar_tensor_tensor(out=decay[:, :, :], in0=ab[:, :, 0:8], scalar=0.0, in1=sp_a[:, :, :],
                                                   op0=ALU.max, op1=ALU.add).then_inc(gate_chain, 1)
                    dve.wait_ge(gate_chain, 6)
                    nc.vector.scalar_tensor_tensor(out=decay[:, :, :], in0=decay[:, :, :], scalar=-1.0,
                                                   in1=ea[:, :].unsqueeze(1).to_broadcast([P, STEPS, 8]),
                                                   op0=ALU.mult, op1=ALU.mult).then_inc(gates_ready, 1)
                    dve.wait_ge(cum_read, 1)
                    cols = lambda b: banks_of(x)[:, b:b + 48].rearrange("p (t c) -> p t c", c=8)
                    nc.vector.tensor_copy(gc[:, :, :], cols(0)).then_inc(cum_scaled, 1)
                    dve.wait_ge(cum_scaled, 1)
                    nc.vector.tensor_tensor(kdec[:, :, :], cols(48), gc[:, :, :], ALU.subtract).then_inc(cum_scaled, 1)
                    nc.vector.scalar_tensor_tensor(out=nbe[:, :, :], in0=beta[:, :, :], scalar=-1.0, in1=eg[:, :, :],
                                                   op0=ALU.mult, op1=ALU.mult).then_inc(cum_read, 1)
                elif x[0] == "dnA":
                    d, n, tile, b = x[2], group(x), SCAN[x[2]][x[1]], work(x)
                    dve.wait_ge(product_done, i + 1)
                    nc.vector.tensor_tensor(dE[b][:, :, :], pair4(banks_of(x), 0), per_head(gc, tile, d),
                                            ALU.subtract).then_inc(dif_done, 1)
                    if d == 1:
                        for y in range(2):
                            a_matrix(("dnA", x[1], y))
                elif x[0] == "dnT":
                    d, n, b = x[2], group(x), work(x)
                    dve.wait_ge(product_done, i + 1)
                    dve.wait_ge(eq_ready, n + 1)
                    nc.vector.tensor_tensor(dQK[b][:, :, :], pair4(banks_of(x), 1), dEQ[b][:, :, :], ALU.mult).then_inc(qk_ready, 1)
                elif x[0] == "dnN":
                    d, k, b = x[2], x[3], work(x)
                    dve.wait_ge(product_done, i + 1)
                    nc.vector.tensor_tensor(dN[b][:, :, :], pair4(banks_of(x), 0), over_heads(LEVEL[d] + k), ALU.mult).then_inc(n_ready, 1)
                elif x[0] == "dnX":
                    dve.wait_ge(product_done, i + 1)
                    nc.vector.tensor_copy(dX[work(x)][:, :, :], pair4(banks_of(x), 0)).then_inc(x_ready, 1)
                elif x[0] == "dnV":
                    d, tile, b = x[2], SCAN[x[2]][x[1]], work(x)
                    dve.wait_ge(product_done, i + 1)
                    nc.vector.tensor_tensor(dVb[b][:, :, :], pair4(banks_of(x), 0), per_head(beta, tile, d), ALU.mult).then_inc(vb_ready, 1)
                    dve.wait_ge(cum_scaled, 3)
                    nc.vector.tensor_tensor(dKd[b][:, :, :], pair4(banks_of(x), 1), per_head(kdec, tile, d), ALU.mult).then_inc(kd_ready, 1)
                elif x[0] == "dnK":
                    d, tile, n, b = x[2], SCAN[x[2]][x[1]], group(x), work(x)
                    dve.wait_ge(product_done, i + 1)
                    dve.wait_ge(vb_ready, n + 1)
                    dve.wait_ge(cum_read, 2)
                    for hd in range(4):
                        ins = nc.vector.scalar_tensor_tensor(out=dVb[b][:, hd, :], in0=pair4(banks_of(x), 0)[:, hd, :],
                                                             scalar=nbe[:, tile, 4 * d + hd:4 * d + hd + 1],
                                                             in1=dVb[b][:, hd, :], op0=ALU.mult, op1=ALU.add)
                    ins.then_inc(r_ready, 1)
                elif x[0] == "dnO":
                    d, st, tile, n, b = x[2], x[1], SCAN[x[2]][x[1]], group(x), work(x)
                    oa = o_acc[:, tile, :].rearrange("p (h e) -> p h e", e=P)
                    pair = banks_of(x)
                    first = SCAN[1 - d].index(tile) > st or (SCAN[1 - d].index(tile) == st and d == 0)
                    dve.wait_ge(product_done, i + 1)
                    if st == 0:
                        dve.wait_ge(spilled_by[d], 16 * 8)
                        nc.vector.tensor_copy(dS[d][:, :, :], pair4(pair, 1)).then_inc(s_ready, 1)
                        nc.vector.tensor_copy(oa, pair4(pair, 0)).then_inc(o_ready, 1)
                        continue
                    dve.wait_ge(s_ready, n)
                    for hd in range(4):
                        s_h = dS[d][:, hd, :]
                        ins = nc.vector.scalar_tensor_tensor(out=s_h, in0=s_h, scalar=egl[:, tile, 4 * d + hd:4 * d + hd + 1],
                                                             in1=pair4(pair, 1)[:, hd, :], op0=ALU.mult, op1=ALU.add)
                    ins.then_inc(s_ready, 1)
                    dve.wait_ge(qs_ready, n - 1)
                    if first:
                        nc.vector.tensor_tensor(oa, pair4(pair, 0), dQS[b][:, :, :], ALU.add).then_inc(o_ready, 1)
                    else:
                        dve.wait_ge(o_ready, n)
                        nc.vector.tensor_tensor(oa, oa, dQS[b][:, :, :], ALU.add).then_inc(o_part, 1)
                        dve.wait_ge(o_part, o_part_no[x] + 1)
                        nc.vector.tensor_tensor(oa, pair4(pair, 0), oa, ALU.add).then_inc(o_ready, 1)
                elif x[0] == "dny":
                    t = x[1]
                    if t == 0:
                        for q in range(STEPS):
                            dve.wait_ge(o_squared, q + 1)
                            nc.vector.reduce_sum(oss[:, q, :], cacc[q % 2][:, 0:4 * P].rearrange("p (h e) -> p h e", e=P),
                                                 axis=mybir.AxisListType.X).then_inc(o_summed, 1)
                        dve.wait_ge(o_std, 1)
                        nc.vector.reciprocal(oss[:, :, :], oss[:, :, :]).then_inc(o_inv, 1)
                        dve.wait_ge(o_inv, 1)
                        for q in range(STEPS):
                            oa = o_acc[:, q, :].rearrange("p (h e) -> p h e", e=P)
                            nc.vector.tensor_tensor(oa, oa, oss[:, q, :].unsqueeze(2).to_broadcast([P, 4, P]),
                                                    ALU.mult).then_inc(o_normed, 1)
                    dve.wait_ge(product_done, i + 1)
                    dve.wait_ge(z_loaded[t % 2], 16 * (t // 2 + 1))
                    if t >= 2:
                        dve.wait_ge(dny_lo, t - 1)
                    nc.vector.scalar_tensor_tensor(out=y_tmp(t), in0=pair4(banks_of(x), 0), scalar=dn_w[:, :],
                                                   in1=zt[t % 2].rearrange("p (k q) -> p k q", q=P),
                                                   op0=ALU.mult, op1=ALU.mult).then_inc(dny_read, 1)
                    dve.wait_ge(dny_hi, t + 1)
                    nc.vector.tensor_tensor(ul[:, 4:8, P * t:P * t + P], y_tmp(t), uh[:, 4:8, P * t:P * t + P].bitcast(f32),
                                            ALU.subtract).then_inc(dny_lo, 1)
                elif x[0] == "rope":
                    r = x[1]
                    dve.wait_ge(product_done, i + 1)
                    if r == 0:
                        dve.wait_ge(rope_loaded, 64)
                    dst = sw_k[:, r, 0:T_LAT] if r < 2 else sq_q[:, r - 2, :]
                    xr = rope_x[r % 2][:, :]
                    nc.vector.tensor_tensor(dst, banks_of(x)[:, 0:T_LAT], rope_s[:, :], ALU.mult).then_inc(rope_mul, 1)
                    nc.vector.tensor_tensor(xr, xr, rope_c[:, :], ALU.mult).then_inc(rope_mul, 1)
                    dve.wait_ge(rope_mul, 2 * r + 2)
                    nc.vector.tensor_tensor(dst, dst, xr, ALU.add).then_inc(rope_done, 1)
                elif x[0] == "S":
                    u, a_ = x[1], x[2]
                    n = 2 * u + a_
                    dve.wait_ge(product_done, i + 1)
                    nc.vector.reduce_max(smx[:, u, a_:a_ + 1], banks_of(x)[:, 0:width(u)], axis=mybir.AxisListType.X).then_inc(max_done, 1)
                    dve.wait_ge(max_done, n + 1)
                    if u < 24:
                        nc.vector.tensor_scalar(snb[:, u, a_:a_ + 1], smx[:, u, a_:a_ + 1], -float(HD) ** -0.5, None,
                                                ALU.mult).then_inc(neg_max, 1)
                    else:
                        if n == 48:
                            nc.vector.tensor_scalar(nsink[:, :], rows[:, 24:40], -1.0, None, ALU.mult).then_inc(sink_neg, 1)
                            dve.wait_ge(sink_neg, 1)
                        col = 2 * tile_of(u) + a_
                        nc.vector.tensor_scalar(snb[:, u, a_:a_ + 1], smx[:, u, a_:a_ + 1], -float(HD) ** -0.5,
                                                nsink[:, col:col + 1], ALU.mult, ALU.min).then_inc(neg_max, 1)
                        if a_:
                            dve.wait_ge(neg_max, n + 1)
                            nc.vector.tensor_tensor(ses[:, u, :], snb[:, u, :], rows[:, col + 23:col + 25], ALU.add).then_inc(sink_sum, 1)
                elif x[0] == "PT":
                    u = x[1]
                    dve.wait_ge(product_done, i + 1)
                    if u >= 1:
                        dve.wait_ge(product_done, number[("O", u - 1)] + 1)
                    nc.vector.tensor_copy(probT(u)[:, 0:4, :], banks_of(x)[:, 0:4 * P].rearrange("p (c q) -> p c q", q=P)) \
                        .then_inc(pt_dve, 1)
                elif x[0] == "O":
                    u = x[1]
                    b = block_of(u)
                    den = sden[:, u, :]
                    dve.wait_ge(exp_done, 2 * u + 2)
                    if u >= 24:
                        dve.wait_ge(sink_done, u - 23)
                        nc.vector.tensor_tensor(den, den, ses[:, u, :], ALU.add).then_inc(den_done, 1)
                        dve.wait_ge(den_done, u - 23)
                    nc.vector.reciprocal(srec[:, u, :], den).then_inc(inv_done, 1)
                    dve.wait_ge(inv_done, u + 1)
                    dve.wait_ge(product_done, i + 1)
                    if b >= 2 and (u % 4 if u < 24 else (u - 24) % KD) == 0 and ("Y", b - 2) in number:
                        dve.wait_ge(product_done, number[("Y", b - 2)] + 1)
                    nc.vector.tensor_tensor(otok(b)[:, P * tile_of(u):P * tile_of(u) + P].rearrange("p (a e) -> p a e", e=HD),
                                            banks_of(x)[:, 0:P].rearrange("p (a e) -> p a e", e=HD),
                                            srec[:, u, :].unsqueeze(2).to_broadcast([P, 2, HD]), ALU.mult).then_inc(o_read, 1)
                elif x[0] == "Y":
                    b = x[1]
                    dve.wait_ge(y_hi, b + 1)
                    for k in range(4 if b < 6 else KD):
                        ins = nc.vector.tensor_tensor(y_target(ul, b)[:, k], y_source(banks_of(x), b)[:, k],
                                                      y_target(uh, b)[:, k].bitcast(f32), ALU.subtract)
                    ins.then_inc(y_lo, 1)
                elif x[0] in RESIDUAL:
                    k = x[-1]
                    dve.wait_ge(product_done, i + 1)
                    dve.wait_ge(mod_ready, ada_no[("ada", x[1], gate_term(x), ADA_SPLIT - 1)] + 1)
                    if res_no[x] >= KD:
                        dve.wait_ge(h_updated, res_no[x] - KD + 1)
                    for v, (lo, hi) in enumerate(segs_of(x)):
                        ins = nc.vector.scalar_tensor_tensor(out=h[:, k, lo:hi], in0=banks_of(x)[:, lo:hi],
                                                             scalar=mod[:, x[1], gate_term(x), k, v:v + 1],
                                                             in1=h[:, k, lo:hi], op0=ALU.mult, op1=ALU.add)
                    ins.then_inc(h_updated, 1)
                    if x in squares:
                        m, q = squares[x]
                        if q:
                            add_square(m, q - 1)
                        if q == KD - 1:
                            add_square(m, q)

        @block.tensor
        def _(pe):

            def dense(x, pair, xh, xl, ready=None):
                n = slot_of[x]
                _, K, w = slots[n]
                pe.wait_ge(lo_split, n + 1)
                for k in range(K):
                    if ready:
                        ready(k)
                    for wt, xt, first, last in ((wh, xh, k == 0, False), (wh, xl, False, False),
                                                (wl, xh, False, k == K - 1)):
                        for lo, hi in segs_of(x):
                            ins = nc.tensor.matmul(pair[:, lo:hi], wt[n % SPLIT_SLOTS][:, k * P:(k + 1) * P],
                                                   xt[:, k, lo:hi], start=first, stop=last)
                return ins

            pe.wait_ge(sc_ready, 2)
            fresh_norm = [-1]
            for x in items:
                i = number[x]
                pair = banks_of(x)
                for y in before[x]:
                    for signal in released(y):
                        pe.wait_ge(*signal)
                if x[0] == "ada":
                    n = ada_no[x]
                    pe.wait_ge(*((start_loaded[n], 16) if n < ADA_FIRST else (ada_loaded, 16 * (n - ADA_FIRST + 1))))
                    w = ada_start[n] if n < ADA_FIRST else ada_raw
                    for t in range(2):
                        for k in range(KD):
                            c = (t * KD + k) * P
                            ins = nc.tensor.matmul(pair[:, 2 * t:2 * t + 2], w[:, c:c + P], sc[:, k, :], start=k == 0, stop=k == KD - 1)
                    ins.then_inc(product_done, 1)
                elif x[0] == "norm":
                    pe.wait_ge(sq_summed, KD * (norm_no[x] + 1))
                    pe.wait_ge(const_loaded, CONSTS)
                    for lo, hi in segs_of(x):
                        ins = nc.tensor.matmul(pair[:, lo:hi], mean_w[:, :], sumsq[:, lo:hi], start=True, stop=True)
                    ins.then_inc(product_done, 1)
                elif x[0] == "proj" and x[2] == "ab":
                    n = slot_of[x]
                    pe.wait_ge(lo_split, n + 1)
                    for t in range(STEPS):
                        for k in range(KD):
                            for ut, wt, first, last in ((uh, wh, k == 0, False), (uh, wl, False, False), (ul, wh, False, k == KD - 1)):
                                ins = nc.tensor.matmul(pair[:, 16 * t:16 * t + 16], ut[:, k, P * t:P * t + P],
                                                       wt[n % SPLIT_SLOTS][:, 16 * k:16 * k + 16], start=first, stop=last)
                    ins.then_inc(product_done, 1)
                elif x in slot_of:
                    m = u_source(x)
                    ready = None
                    if x[0] in ("gate", "up", "proj") and fresh_norm[0] != m:
                        fresh_norm[0] = m
                        ready = lambda k: pe.wait_ge(u_lo[k % 2], KD // 2 * m + k // 2 + 1)
                    if x[0] == "down" and x[4] == 0:
                        first = glu_no[next(y for y in items if y[0] == "up" and y[1:4] == x[1:4])[1:]]
                        ready = lambda k: pe.wait_ge(a_lo, first + k + 1)
                    if x[0] == "out" and x[2] == 0:
                        pe.wait_ge(y_lo, 6 if x[1] == 0 else 10)
                        pe.wait_ge(dny_lo, STEPS)
                    src = (ah, al) if x[0] == "down" else (uh, ul)
                    dense(x, pair, *src, ready=ready).then_inc(product_done, 1)
                elif x[0] == "l2":
                    j = no["l2"][x]
                    pe.wait_ge(l2_squared, j + 1)
                    for lo, hi in (LAT, CTX):
                        ins = nc.tensor.matmul(pair[:, lo:hi], ones_w[:, :], sq[j % 2][:, lo:hi], start=True, stop=True)
                    ins.then_inc(product_done, 1)
                elif x[0] == "cum":
                    pe.wait_ge(gates_ready, 1)
                    pe.wait_ge(masks_loaded, 16)
                    cols = lambda b: pair[:, b:b + 48].rearrange("p (t c) -> p t c", c=8)
                    for d in range(2):
                        nc.tensor.matmul(cols(0)[:, :, 4 * d:4 * d + 4], masks[:, U[d], :], decay[:, :, 4 * d:4 * d + 4],
                                         start=True, stop=True)
                    nc.tensor.matmul(pair[:, 48:96], ones_w[:, :], decay[:, :, :].rearrange("p t c -> p (t c)"),
                                     start=True, stop=True).then_inc(product_done, 1)
                elif x[0] == "dnA":
                    d, tile, b = x[2], SCAN[x[2]][x[1]], work(x)
                    if x[1] == 0:
                        pe.wait_ge(l2_done, 8)
                        pe.wait_ge(cum_read, 2)
                    kT = dqkv[:, 1, :, P * tile:P * tile + P]
                    for hd in range(4):
                        c = 4 * d + hd
                        nc.tensor.matmul(pair4(pair, 0)[:, hd, :], decay[:, tile, c:c + 1].to_broadcast([P, P]), masks[:, U[d], :],
                                         start=True, stop=True)
                    for hd in range(4):
                        ins = nc.tensor.matmul(pair4(pair, 1)[:, hd, :], kT[:, hd, :], kT[:, hd, :], start=True, stop=True)
                    ins.then_inc(product_done, 1)
                elif x[0] == "dnT":
                    d, tile, b = x[2], SCAN[x[2]][x[1]], work(x)
                    for hd in range(4):
                        nc.tensor.matmul(pair4(pair, 1)[:, hd, :], dqkv[:, 1, hd, P * tile:P * tile + P],
                                         dqkv[:, 0, hd, P * tile:P * tile + P], start=True, stop=True)
                    pe.wait_ge(a_ready, group(x) + 1)
                    for hd in range(4):
                        ins = nc.tensor.transpose(pair4(pair, 0)[:, hd, :], dA[b][:, hd, :], ident[:, :])
                    ins.then_inc(product_done, 1)
                elif x[0] == "dnN":
                    d, k, n, b = x[2], x[3], group(x), work(x)
                    if k == 1:
                        pe.wait_ge(at_ready, n + 1)
                        pe.wait_ge(x1_ready, n + 1)
                    else:
                        pe.wait_ge(x_ready, no["dnX"][("dnX", x[1], d, k - 1)] + 1)
                    for hd in range(4):
                        ins = nc.tensor.matmul(pair4(pair, 0)[:, hd, :], dAT[b][:, hd, :], dX[b][:, hd, :], start=True, stop=True)
                    ins.then_inc(product_done, 1)
                elif x[0] == "dnY":
                    d, k, n, b = x[2], x[3], group(x), work(x)
                    pe.wait_ge(n_ready, no["dnN"][("dnN",) + x[1:]] + 1)
                    if k == 1:
                        pe.wait_ge(y1_ready, n + 1)
                    for hd in range(4):
                        ins = nc.tensor.matmul(pair4(pair, 0)[:, hd, :], dN[b][:, hd, :], dY[b][:, hd, :], start=True, stop=True)
                    ins.then_inc(product_done, 1)
                elif x[0] == "dnX":
                    b = work(x)
                    pe.wait_ge(y_ready, no["dnY"][("dnY",) + x[1:]] + 1)
                    for hd in range(4):
                        ins = nc.tensor.transpose(pair4(pair, 0)[:, hd, :], dY[b][:, hd, :], ident[:, :])
                    ins.then_inc(product_done, 1)
                elif x[0] == "dnV":
                    tile = SCAN[x[2]][x[1]]
                    for w, half in ((2, 0), (1, 1)):
                        for hd in range(4):
                            ins = nc.tensor.transpose(pair4(pair, half)[:, hd, :], dqkv[:, w, hd, P * tile:P * tile + P], ident[:, :])
                    ins.then_inc(product_done, 1)
                elif x[0] == "dnK":
                    d, tile, n, b = x[2], SCAN[x[2]][x[1]], group(x), work(x)
                    pe.wait_ge(s_ready, n - 1)
                    for w, half in ((1, 0), (0, 1)):
                        for hd in range(4):
                            ins = nc.tensor.matmul(pair4(pair, half)[:, hd, :], dqkv[:, w, hd, P * tile:P * tile + P],
                                                   dS[d][:, hd, :], start=True, stop=True)
                    ins.then_inc(product_done, 1)
                elif x[0] == "dnU":
                    d, n, b = x[2], group(x), work(x)
                    if x[1]:
                        pe.wait_ge(r_ready, n - 1)
                    pe.wait_ge(vb_ready, n + 1)
                    pe.wait_ge(y_ready, no["dnY"][("dnY", x[1], d, LEVELS - 1)] + 1)
                    for hd in range(4):
                        ins = nc.tensor.matmul(pair4(pair, 0)[:, hd, :], dY[b][:, hd, :], dVb[b][:, hd, :],
                                               start=True, stop=True)
                    ins.then_inc(product_done, 1)
                elif x[0] == "dnO":
                    d, n, b = x[2], group(x), work(x)
                    pe.wait_ge(vn_ready, n + 1)
                    pe.wait_ge(qk_ready, n + 1)
                    pe.wait_ge(kd_ready, n + 1)
                    for lhs, half in ((dQK, 0), (dKd, 1)):
                        for hd in range(4):
                            ins = nc.tensor.matmul(pair4(pair, half)[:, hd, :], lhs[b][:, hd, :], dVn[b][:, hd, :],
                                                   start=True, stop=True)
                    ins.then_inc(product_done, 1)
                elif x[0] == "dny":
                    pe.wait_ge(o_normed, x[1] + 1)
                    for hd in range(4):
                        ins = nc.tensor.transpose(pair4(pair, 0)[:, hd, :], o_acc[:, x[1], P * hd:P * hd + P], ident[:, :])
                    ins.then_inc(product_done, 1)
                elif x[0] == "vt":
                    if x == ("vt", 0, 4):
                        pe.wait_ge(na_loaded, 48)
                    if x[1] == 0 and x[2] < 4:
                        pe.wait_ge(v_gathered, x[2] + 1)
                    if x[1] == 0:
                        for c in range(2):
                            for f in range(4):
                                v = nqkv[:, 2, f, :]
                                if x[2] == 4:
                                    src = v[:, T_LAT + P * c:T_LAT + P * c + P]
                                else:
                                    src = v_cols(f)[:, P * c:P * c + P]
                                ins = nc.tensor.transpose(pair[:, 512 * c + P * f:512 * c + P * f + P], src, ident[:, :])
                    else:
                        pe.wait_ge(odd_read, odd_no[("proj", 1, "v", 1)] + 1)
                        for t in range(3):
                            for f in range(2):
                                m = 3 * x[2] + t
                                ins = nc.tensor.transpose(pair[:, 256 * t + P * f:256 * t + P * f + P],
                                                          sw_v[:, f, P * m:P * m + P], ident[:, :])
                    ins.then_inc(product_done, 1)
                elif x[0] == "rope":
                    r = x[1]
                    pe.wait_ge(odd_read, odd_no[rope_items[r]] + 1)
                    pe.wait_ge(rope_loaded, 64)
                    nc.tensor.matmul(pair[:, 0:T_LAT], rope_p[:, :], rope_x[r % 2][:, :], start=True, stop=True) \
                        .then_inc(product_done, 1)
                elif x[0] == "S":
                    u, a_ = x[1], x[2]
                    q, keys, _ = attention(u, a_)
                    if u == 0:
                        pe.wait_ge(na_loaded, 48)
                    if u < 16:
                        pe.wait_ge(bias_ready, u + 1)
                    if u == 24:
                        pe.wait_ge(rope_done, 10)
                    for col, n, k, extra in keys:
                        ins = nc.tensor.matmul(pair[:, col:col + n], q, k, start=True, stop=extra is None)
                        if extra is not None:
                            ins = nc.tensor.matmul(pair[:, col:col + n], ident[:, :], extra, start=False, stop=True)
                    ins.then_inc(product_done, 1)
                elif x[0] == "PT":
                    u, n = x[1], width(x[1]) // P
                    for a_ in range(2):
                        pe.wait_ge(exp_done, 2 * u + a_ + 1)
                        for c in range(n):
                            ins = nc.tensor.transpose(pair[:, P * (n * a_ + c):P * (n * a_ + c + 1)],
                                                      prob(u, a_)[:, P * c:P * c + P], ident[:, :])
                    ins.then_inc(product_done, 1)
                elif x[0] == "O":
                    u = x[1]
                    for signal in released(("PT", u)):
                        pe.wait_ge(*signal)
                    pe.wait_ge(v_read, 7 if u >= 24 else 5 if u >= 12 else u // 4 + 2)
                    for a_ in range(2):
                        vs = attention(u, a_)[2]
                        for c, v in enumerate(vs):
                            ins = nc.tensor.matmul(pair[:, HD * a_:HD * a_ + HD], probT(u)[:, len(vs) * a_ + c, :], v,
                                                   start=c == 0, stop=c == len(vs) - 1)
                    ins.then_inc(product_done, 1)
                elif x[0] == "Y":
                    b = x[1]
                    pe.wait_ge(o_read, 4 * b + 4 if b < 6 else 24 + KD * (b - 5))
                    for k in range(4 if b < 6 else KD):
                        ins = nc.tensor.transpose(pair[:, P * k:P * k + P], otok(b)[:, P * k:P * k + P], ident[:, :])
                    ins.then_inc(product_done, 1)


def feature_major(v):
    return v.reshape(-1, P, v.shape[-1]).transpose(1, 0, 2)


def weight_of(x, n, inputs):
    if x[0] in ("gate", "up"):
        w = inputs["ffn_w_up"][x[1], x[2]]
        c = x[5] * P + (D_FF if x[0] == "up" else 0)
        return w[:, c:c + P]
    if x[0] == "down":
        r = sum(PARTS[:x[3]]) * P
        return inputs["ffn_w_down"][x[1], x[2]][r:r + PARTS[x[3]] * P, x[4] * P:(x[4] + 1) * P]
    return mixer_weight(x, inputs)


def query_heads(t):
    per = SWA_HEADS // SWA_KV
    return [(2 * (t // per) + a) * per + t % per for a in range(2)]


def mixer_weight(x, inputs):
    if x[0] == "proj" and x[1] == 0:
        w, i = inputs["even_w_in"][0], x[3]
        first = {"nq": 0, "nk": 512, "nv": 1024, "dq": NA_PROJ, "dk": NA_PROJ + 512, "dv": NA_PROJ + 1024,
                 "z": NA_PROJ + DN_QKV, "ab": NA_PROJ + DN_QKV + DN_HEADS * P}[x[2]]
        return w[:, first + P * i:first + (16 if x[2] == "ab" else P * i + P)]
    if x[0] == "proj":
        w, i = inputs["odd_w_in"][0], x[3]
        if x[2] == "q":
            return np.concatenate([w[:, HD * q:HD * q + HD] for q in query_heads(i)], 1)
        first = SWA_HEADS * HD + (0 if x[2] == "k" else SWA_KV * HD)
        return w[:, first + P * i:first + P * i + P]
    cols = slice(P * x[2], P * x[2] + P)
    if x[1] == 0:
        return inputs["even_w_out"][0][:, cols]
    w = inputs["odd_w_out"][0]
    return np.concatenate([w[HD * q:HD * q + HD, cols] for t in range(KD) for q in query_heads(t)], 0)


def constants():
    i, j = np.arange(P)[:, None], np.arange(P)[None, :]
    f = lambda x: np.asarray(x, np.float32)
    level = lambda b: f(i == j) - f((i // b == j // b + 1) & ((j // b) % 2 == 0))
    lower = [level(2 ** k) for k in range(LEVELS)]
    masks = [f(i <= j), f(i >= j), f(i > j), f(i < j)] + lower + [m.T for m in lower]
    m8 = []
    for jb in (0, 1, 3):
        qc = 16 * jb + np.arange(16)
        kc = min(max(16 * jb - 8, 0), 32) + np.arange(32)
        start = np.clip(qc - 8, 0, 48)[:, None]
        ok = (kc >= start) & (kc < start + 16)
        m8.append(np.tile(np.where(ok, 0.0, NEG * HD ** 0.5), (ROWS, ROWS)))
    wmask = [np.where(j >= i, 0.0, NEG * HD ** 0.5), np.where(j <= i, 0.0, NEG * HD ** 0.5)]
    t = np.arange(T_LAT)
    inv = np.power(np.float32(10000.0), -np.arange(0, 32, 2, dtype=np.float32) / np.float32(32))
    feat = np.arange(P) % HD
    pos = np.where((feat < 32)[:, None], t // GRID_W, t % GRID_W).astype(np.float32)
    ang = pos * inv[feat % 16][:, None]
    sign = np.where(feat % 32 < 16, -1.0, 1.0)[:, None]
    return {
        "masks": f(np.stack(masks, 1)), "m8": f(np.stack(m8, 1)), "wmask": f(np.stack(wmask, 1)),
        "rope_c": f(np.cos(ang)), "rope_s": f(np.sin(ang) * sign), "rope_p": f(j == (i ^ 16)),
        "ident": np.eye(P, dtype=np.float32), "ones_w": np.ones((P, P), np.float32),
        "mean_w": np.full((P, P), 1.0 / D, np.float32),
    }


def layouts(inputs, items):
    x = np.concatenate([inputs["x"][0], inputs["ctx"][0]], 0).T
    cs = np.stack([inputs["c"][0], inputs["c_ctx"]], 1)
    ada = inputs["ada_w"].reshape(DEPTH, KD, P, N_MOD, ADA_SPLIT, 2, P).transpose(0, 3, 4, 2, 5, 1, 6)
    gs = np.concatenate([inputs["norm_g"].reshape(DEPTH * 3, D), inputs["final_norm_g"][None]], 0)
    parts = [feature_major(weight_of(y, n, inputs)).reshape(-1) for n, (y, _, _) in enumerate(weight_slots(items))]
    return {
        "xT": feature_major(x),
        "cT": feature_major(cs),
        "ada_w": ada.reshape(DEPTH, N_MOD, ADA_SPLIT, P, 2 * KD * P),
        "ada_bT": inputs["ada_b"].reshape(DEPTH, N_MOD, KD, P).transpose(3, 0, 1, 2),
        "norm_gT": gs.reshape(-1, KD, P).transpose(2, 0, 1),
        "rows": np.concatenate([inputs["dn_a_log"][0].reshape(-1), inputs["dn_dt_bias"][0].reshape(-1), np.zeros(8, np.float32),
                                np.concatenate([inputs["swa_sink"][0][query_heads(t)] for t in range(KD)])])[None],
        "conv_w": inputs["dn_conv_w"][0].reshape(CONV, 12, P).transpose(2, 1, 0),
        "dn_w": inputs["dn_norm_w"][0][:, None],
        "rpb": np.pad(inputs["na_rpb"][0], ((0, 0), (0, 0), (16, 16))),
        "w": np.concatenate(parts),
        **constants(),
    }


def kernel(**inputs):
    import concourse.bacc as bacc
    from concourse.bass_utils import run_bass_kernel_spmd

    inputs = {k: np.asarray(v) for k, v in inputs.items()}
    items = schedule()
    arrays = {k: np.ascontiguousarray(v) for k, v in layouts(inputs, items).items()}
    nc = bacc.Bacc("TRN2", target_bir_lowering=False, num_devices=1)
    aps = {k: nc.dram_tensor(f"in_{k}", v.shape, mybir.dt.from_np(v.dtype), kind="ExternalInput").ap()
           for k, v in arrays.items()}
    out = nc.dram_tensor("out_h", (KD, P, T_LAT), mybir.dt.float32, kind="ExternalOutput").ap()
    build(nc, aps, out, items)
    r = run_bass_kernel_spmd(nc, [{f"in_{k}": v for k, v in arrays.items()}], core_ids=[0])
    return r.results[0]["out_h"].transpose(2, 0, 1).reshape(1, T_LAT, D)
```
